# Optimizing a Trainium2 kernel written in Bass

```python
import jax, jax.numpy as jnp
from jax import lax
import numpy as np

D_MODEL = 1024
BATCH = 1
SEQ = 256
DEPTH = 2

GRID_W = 64
CTX_LEN = 256
EPS = 1e-6
ROPE_BASE = 10000.0
NEG_INF = -1e30

GLA_HEADS = 4
GLA_HEAD_K = D_MODEL // (2 * GLA_HEADS)
GLA_HEAD_V = D_MODEL // GLA_HEADS
GLA_QK = GLA_HEADS * GLA_HEAD_K
GLA_V = GLA_HEADS * GLA_HEAD_V
GLA_RANK = 16
GLA_GATE_NORM = 16.0
GLA_CHUNK = 64

SWA_HEADS = 8
SWA_KV_HEADS = 2
SWA_GROUP = SWA_HEADS // SWA_KV_HEADS
SWA_HEAD_DIM = D_MODEL // SWA_HEADS
SWA_WINDOW = 128
SWA_BLOCK = 128
SWA_SCALE = SWA_HEAD_DIM ** -0.5

MLA_HEADS = 8
MLA_Q_RANK = 384
MLA_KV_RANK = 256
MLA_NOPE = 128
MLA_ROPE = 64
MLA_V = D_MODEL // MLA_HEADS
MLA_QUERY_BLOCK = 128
MLA_SCALE = (MLA_NOPE + MLA_ROPE) ** -0.5

N_BRANCH = 3
BRANCH_W = D_MODEL
FF_DIM = 4 * D_MODEL

IN_SIZES = (GLA_QK, GLA_QK, GLA_V, GLA_V, GLA_RANK, GLA_RANK,
            SWA_HEADS * SWA_HEAD_DIM, SWA_KV_HEADS * SWA_HEAD_DIM, SWA_KV_HEADS * SWA_HEAD_DIM,
            MLA_Q_RANK, MLA_KV_RANK, MLA_ROPE, N_BRANCH * D_MODEL)
IN_WIDTH = sum(IN_SIZES)
IN_OFFSETS = tuple(int(v) for v in np.cumsum(IN_SIZES)[:-1])

kernel_name = 'hybrid_gla_swa_mla_prefix_dit'

def rms_norm(x, w):
    xf = x.astype(jnp.float32)
    y = xf * lax.rsqrt(jnp.mean(xf * xf, axis=-1, keepdims=True) + EPS)
    return (y * w.astype(jnp.float32)).astype(x.dtype)

def modulate(x, w, shift, scale):
    return rms_norm(x, w) * (1 + scale[..., None, :]) + shift[..., None, :]

def squared_relu_mlp(h, w1, w2):
    return jnp.square(jax.nn.relu(h @ w1)) @ w2

def axial_tables(row, col, dim, dtype):
    d_axis = dim // 2
    inv = ROPE_BASE ** (-jnp.arange(0, d_axis, 2, dtype=jnp.float32) / d_axis)
    ang_r = row.astype(jnp.float32)[:, None] * inv
    ang_c = col.astype(jnp.float32)[:, None] * inv
    return tuple(t[:, None, :].astype(dtype) for t in (jnp.cos(ang_r), jnp.sin(ang_r), jnp.cos(ang_c), jnp.sin(ang_c)))

def rope_rotate(x, cos, sin):
    x1, x2 = jnp.split(x, 2, axis=-1)
    return jnp.concatenate([x1 * cos - x2 * sin, x2 * cos + x1 * sin], axis=-1)

def apply_axial(x, tabs):
    cos_r, sin_r, cos_c, sin_c = tabs
    x_row, x_col = jnp.split(x, 2, axis=-1)
    return jnp.concatenate([rope_rotate(x_row, cos_r, sin_r), rope_rotate(x_col, cos_c, sin_c)], axis=-1)

def to_heads(t, n_heads):
    b, t_len, _ = t.shape
    return t.reshape(b, t_len, n_heads, -1).transpose(0, 2, 1, 3)

def from_heads(t):
    b, h, t_len, d = t.shape
    return t.transpose(0, 2, 1, 3).reshape(b, t_len, h * d)

def gla_log_decay(z, a_w, a_b):
    return jax.nn.log_sigmoid((z @ a_w + a_b).astype(jnp.float32)) / GLA_GATE_NORM

def gla_chunked(q, k, v, log_a, s0):
    b_, h_, t_len, dk = q.shape
    dv = v.shape[-1]
    n = t_len // GLA_CHUNK
    f32 = jnp.float32
    qc = q.astype(f32).reshape(b_, h_, n, GLA_CHUNK, dk)
    kc = k.astype(f32).reshape(b_, h_, n, GLA_CHUNK, dk)
    vc = v.astype(f32).reshape(b_, h_, n, GLA_CHUNK, dv)
    bcum = jnp.cumsum(log_a.astype(f32).reshape(b_, h_, n, GLA_CHUNK, dk), axis=3)
    b_last = bcum[:, :, :, -1:, :]
    q_dec = qc * jnp.exp(bcum)
    k_inv = kc * jnp.exp(-bcum)
    k_end = kc * jnp.exp(b_last - bcum)
    causal = jnp.tril(jnp.ones((GLA_CHUNK, GLA_CHUNK), bool))
    a_intra = jnp.where(causal, jnp.einsum('bhnid,bhnjd->bhnij', q_dec, k_inv), 0.0)
    o_intra = jnp.einsum('bhnij,bhnjv->bhniv', a_intra, vc)
    u = jnp.einsum('bhncd,bhncv->bhndv', k_end, vc)
    g = jnp.exp(b_last[:, :, :, 0, :])

    def step(s, inp):
        g_n, u_n = inp
        return g_n[..., None] * s + u_n, s

    s_final, s_prev = lax.scan(step, s0, (jnp.moveaxis(g, 2, 0), jnp.moveaxis(u, 2, 0)))
    o_inter = jnp.einsum('bhncd,nbhdv->bhncv', q_dec, s_prev)
    o = (o_intra + o_inter).reshape(b_, h_, t_len, dv).astype(v.dtype)
    return o, s_final

def gla_bidirectional(q, k, v, la_f, la_b, s0_f, s0_b):
    o_f, s_f = gla_chunked(q, k, v, la_f, s0_f)
    flip = lambda t: jnp.flip(t, axis=2)
    o_b, s_b = gla_chunked(flip(q), flip(k), flip(v), flip(la_b), s0_b)
    return o_f + flip(o_b), s_f, s_b

def gla_output(o, r, norm_w):
    return from_heads(rms_norm(o, norm_w)) * jax.nn.silu(r)

def swa_latent(q, k, v, k_ctx, v_ctx, sink):
    b_, t_len = q.shape[0], q.shape[1]
    nb = t_len // SWA_BLOCK
    qb = q.reshape(b_, nb, SWA_BLOCK, SWA_KV_HEADS, SWA_GROUP, SWA_HEAD_DIM)

    def band(t):
        pad = jnp.zeros((b_, SWA_BLOCK) + t.shape[2:], t.dtype)
        tp = jnp.concatenate([pad, t, pad], axis=1).reshape((b_, nb + 2, SWA_BLOCK) + t.shape[2:])
        return jnp.concatenate([tp[:, :-2], tp[:, 1:-1], tp[:, 2:]], axis=2)

    kb, vb = band(k), band(v)
    blk = jnp.arange(nb)[:, None, None]
    q_pos = blk * SWA_BLOCK + jnp.arange(SWA_BLOCK)[None, :, None]
    k_pos = (blk - 1) * SWA_BLOCK + jnp.arange(3 * SWA_BLOCK)[None, None, :]
    valid = (jnp.abs(q_pos - k_pos) <= SWA_WINDOW) & (k_pos >= 0) & (k_pos < t_len)
    s_loc = jnp.einsum('bnqkgd,bnskd->bkgnqs', qb, kb, preferred_element_type=jnp.float32) * SWA_SCALE
    s_loc = jnp.where(valid, s_loc, NEG_INF)
    s_ctx = jnp.einsum('bnqkgd,bskd->bkgnqs', qb, k_ctx, preferred_element_type=jnp.float32) * SWA_SCALE
    sink_col = jnp.broadcast_to(sink.astype(jnp.float32).reshape(1, SWA_KV_HEADS, SWA_GROUP, 1, 1, 1),
                                s_loc.shape[:-1] + (1,))
    p = jax.nn.softmax(jnp.concatenate([s_loc, s_ctx, sink_col], axis=-1), axis=-1).astype(v.dtype)
    n_loc = 3 * SWA_BLOCK
    o = (jnp.einsum('bkgnqs,bnskd->bnqkgd', p[..., :n_loc], vb)
         + jnp.einsum('bkgnqs,bskd->bnqkgd', p[..., n_loc:n_loc + k_ctx.shape[1]], v_ctx))
    return o.reshape(b_, t_len, SWA_HEADS * SWA_HEAD_DIM)

def swa_context(q, k, v, sink):
    b_, l_c = q.shape[0], q.shape[1]
    qg = q.reshape(b_, l_c, SWA_KV_HEADS, SWA_GROUP, SWA_HEAD_DIM)
    s = jnp.einsum('bqkgd,bskd->bkgqs', qg, k, preferred_element_type=jnp.float32) * SWA_SCALE
    sink_col = jnp.broadcast_to(sink.astype(jnp.float32).reshape(1, SWA_KV_HEADS, SWA_GROUP, 1, 1),
                                s.shape[:-1] + (1,))
    p = jax.nn.softmax(jnp.concatenate([s, sink_col], axis=-1), axis=-1).astype(v.dtype)
    o = jnp.einsum('bkgqs,bskd->bqkgd', p[..., :l_c], v)
    return o.reshape(b_, l_c, SWA_HEADS * SWA_HEAD_DIM)

def mla_keys(c_kv, k_rope, norm_w, w_ukv, rope):
    b_, t_len, _ = c_kv.shape
    kv = (rms_norm(c_kv, norm_w) @ w_ukv).reshape(b_, t_len, MLA_HEADS, MLA_NOPE + MLA_V)
    k_nope, v = jnp.split(kv, [MLA_NOPE], axis=-1)
    k_pe = k_rope[:, :, None, :]
    if rope is not None:
        k_pe = apply_axial(k_pe, rope)
    k = jnp.concatenate([k_nope, jnp.broadcast_to(k_pe, (b_, t_len, MLA_HEADS, MLA_ROPE))], axis=-1)
    return k, v

def mla_queries(c_q, norm_w, w_uq, rope):
    b_, t_len, _ = c_q.shape
    q = (rms_norm(c_q, norm_w) @ w_uq).reshape(b_, t_len, MLA_HEADS, MLA_NOPE + MLA_ROPE)
    if rope is not None:
        q_nope, q_pe = jnp.split(q, [MLA_NOPE], axis=-1)
        q = jnp.concatenate([q_nope, apply_axial(q_pe, rope)], axis=-1)
    return q

def dense_attention(q, k, v, scale):
    b_, t_len, h_, dq = q.shape
    nb = t_len // MLA_QUERY_BLOCK
    qb = q.reshape(b_, nb, MLA_QUERY_BLOCK, h_, dq).transpose(1, 0, 2, 3, 4)

    def attend_block(q_blk):
        s = jnp.einsum('bqhd,bshd->bhqs', q_blk, k, preferred_element_type=jnp.float32) * scale
        p = jax.nn.softmax(s, axis=-1).astype(v.dtype)
        return jnp.einsum('bhqs,bshv->bqhv', p, v)

    o = lax.map(attend_block, qb)
    return o.transpose(1, 0, 2, 3, 4).reshape(b_, t_len, h_ * v.shape[-1])

def merge_branches(gates, o_gla, o_swa, o_mla, w_branch, w_out):
    g = jax.nn.sigmoid(gates.reshape(gates.shape[:-1] + (N_BRANCH, D_MODEL)))
    merged = (g[..., 0, :] * (o_gla @ w_branch[0])
              + g[..., 1, :] * (o_swa @ w_branch[1])
              + g[..., 2, :] * (o_mla @ w_branch[2]))
    return merged @ w_out

def token_mixers(h, hc, w_in, gla_a_w, gla_a_b, gla_norm_w, swa_sink, mla_q_norm_w, mla_w_uq,
                 mla_kv_norm_w, mla_w_ukv, w_branch, w_out, rope_swa, rope_mla, with_ctx_out):
    b_, t_len, _ = h.shape
    l_c = hc.shape[1]
    (gq, gk, gv, gr, gzf, gzb, sq, sk, sv, mcq, mckv, mkr, gates) = jnp.split(h @ w_in, IN_OFFSETS, axis=-1)
    (cgq, cgk, cgv, cgr, cgzf, cgzb, csq, csk, csv, cmcq, cmckv, cmkr, cgates) = jnp.split(hc @ w_in, IN_OFFSETS, axis=-1)

    def gla_inputs(q, k, v, zf, zb):
        return (to_heads(q * GLA_HEAD_K ** -0.5, GLA_HEADS), to_heads(k, GLA_HEADS), to_heads(v, GLA_HEADS),
                to_heads(gla_log_decay(zf, gla_a_w[0], gla_a_b[0]), GLA_HEADS),
                to_heads(gla_log_decay(zb, gla_a_w[1], gla_a_b[1]), GLA_HEADS))

    s0 = jnp.zeros((b_, GLA_HEADS, GLA_HEAD_K, GLA_HEAD_V), jnp.float32)
    o_gc, s_f, s_b = gla_bidirectional(*gla_inputs(cgq, cgk, cgv, cgzf, cgzb), s0, s0)
    o_g, _, _ = gla_bidirectional(*gla_inputs(gq, gk, gv, gzf, gzb), s_f, s_b)
    o_gla = gla_output(o_g, gr, gla_norm_w)

    q_s = apply_axial(sq.reshape(b_, t_len, SWA_HEADS, SWA_HEAD_DIM), rope_swa)
    k_s = apply_axial(sk.reshape(b_, t_len, SWA_KV_HEADS, SWA_HEAD_DIM), rope_swa)
    v_s = sv.reshape(b_, t_len, SWA_KV_HEADS, SWA_HEAD_DIM)
    k_sc = csk.reshape(b_, l_c, SWA_KV_HEADS, SWA_HEAD_DIM)
    v_sc = csv.reshape(b_, l_c, SWA_KV_HEADS, SWA_HEAD_DIM)
    o_swa = swa_latent(q_s, k_s, v_s, k_sc, v_sc, swa_sink)

    k_m, v_m = mla_keys(mckv, mkr, mla_kv_norm_w, mla_w_ukv, rope_mla)
    k_mc, v_mc = mla_keys(cmckv, cmkr, mla_kv_norm_w, mla_w_ukv, None)
    q_m = mla_queries(mcq, mla_q_norm_w, mla_w_uq, rope_mla)
    o_mla = dense_attention(q_m, jnp.concatenate([k_m, k_mc], axis=1), jnp.concatenate([v_m, v_mc], axis=1), MLA_SCALE)

    y = merge_branches(gates, o_gla, o_swa, o_mla, w_branch, w_out)
    if not with_ctx_out:
        return y, None

    o_gla_c = gla_output(o_gc, cgr, gla_norm_w)
    o_swa_c = swa_context(csq.reshape(b_, l_c, SWA_HEADS, SWA_HEAD_DIM), k_sc, v_sc, swa_sink)
    o_mla_c = dense_attention(mla_queries(cmcq, mla_q_norm_w, mla_w_uq, None), k_mc, v_mc, MLA_SCALE)
    yc = merge_branches(cgates, o_gla_c, o_swa_c, o_mla_c, w_branch, w_out)
    return y, yc

def setup_inputs(seed: int = 0) -> dict:
    key = jax.random.key(seed)
    ks = jax.random.split(key, 22)
    f32 = jnp.float32

    def dense(k, shape, fan_in):
        return jax.random.normal(k, shape, f32) * fan_in ** -0.5

    def gain(k, shape):
        return 1.0 + 0.02 * jax.random.normal(k, shape, f32)

    return {
        'x': jax.random.normal(ks[0], (BATCH, SEQ, D_MODEL), f32),
        'c': jax.random.normal(ks[1], (BATCH, D_MODEL), f32),
        'ctx': jax.random.normal(ks[2], (BATCH, CTX_LEN, D_MODEL), f32),
        'c_ctx': jax.random.normal(ks[3], (D_MODEL,), f32),
        'ada_w': dense(ks[4], (DEPTH, D_MODEL, 6 * D_MODEL), D_MODEL),
        'ada_b': 0.02 * jax.random.normal(ks[5], (DEPTH, 6 * D_MODEL), f32),
        'norm_mix_w': gain(ks[6], (DEPTH, D_MODEL)),
        'w_in': dense(ks[7], (DEPTH, D_MODEL, IN_WIDTH), D_MODEL),
        'gla_a_w': dense(ks[8], (DEPTH, 2, GLA_RANK, GLA_QK), GLA_RANK),
        'gla_a_b': 0.1 * jax.random.normal(ks[9], (DEPTH, 2, GLA_QK), f32),
        'gla_norm_w': gain(ks[10], (DEPTH, GLA_HEAD_V)),
        'swa_sink': 0.5 * jax.random.normal(ks[11], (DEPTH, SWA_HEADS), f32),
        'mla_q_norm_w': gain(ks[12], (DEPTH, MLA_Q_RANK)),
        'mla_w_uq': dense(ks[13], (DEPTH, MLA_Q_RANK, MLA_HEADS * (MLA_NOPE + MLA_ROPE)), MLA_Q_RANK),
        'mla_kv_norm_w': gain(ks[14], (DEPTH, MLA_KV_RANK)),
        'mla_w_ukv': dense(ks[15], (DEPTH, MLA_KV_RANK, MLA_HEADS * (MLA_NOPE + MLA_V)), MLA_KV_RANK),
        'w_branch': dense(ks[16], (DEPTH, N_BRANCH, BRANCH_W, D_MODEL), BRANCH_W),
        'w_out': dense(ks[17], (DEPTH, D_MODEL, D_MODEL), D_MODEL),
        'norm_mlp_w': gain(ks[18], (DEPTH, D_MODEL)),
        'mlp_w1': dense(ks[19], (DEPTH, D_MODEL, FF_DIM), D_MODEL),
        'mlp_w2': dense(ks[20], (DEPTH, FF_DIM, D_MODEL), FF_DIM),
        'final_norm_w': gain(ks[21], (D_MODEL,)),
    }

def reference(x, c, ctx, c_ctx, ada_w, ada_b, norm_mix_w, w_in, gla_a_w, gla_a_b, gla_norm_w, swa_sink,
              mla_q_norm_w, mla_w_uq, mla_kv_norm_w, mla_w_ukv, w_branch, w_out, norm_mlp_w, mlp_w1, mlp_w2,
              final_norm_w):
    n_tok = x.shape[1]
    rows = n_tok // GRID_W
    row = jnp.repeat(jnp.arange(rows), GRID_W)
    col = jnp.tile(jnp.arange(GRID_W), rows)
    rope_swa = axial_tables(row, col, SWA_HEAD_DIM, x.dtype)
    rope_mla = axial_tables(row, col, MLA_ROPE, x.dtype)
    xc = ctx
    for layer in range(DEPTH):
        with_ctx_out = layer < DEPTH - 1
        mod = jax.nn.silu(c) @ ada_w[layer] + ada_b[layer]
        mod_c = jax.nn.silu(c_ctx) @ ada_w[layer] + ada_b[layer]
        sh_m, sc_m, g_m, sh_f, sc_f, g_f = jnp.split(mod, 6, axis=-1)
        csh_m, csc_m, cg_m, csh_f, csc_f, cg_f = jnp.split(mod_c, 6, axis=-1)
        y, yc = token_mixers(modulate(x, norm_mix_w[layer], sh_m, sc_m),
                             modulate(xc, norm_mix_w[layer], csh_m, csc_m),
                             w_in[layer], gla_a_w[layer], gla_a_b[layer], gla_norm_w[layer], swa_sink[layer],
                             mla_q_norm_w[layer], mla_w_uq[layer], mla_kv_norm_w[layer], mla_w_ukv[layer],
                             w_branch[layer], w_out[layer], rope_swa, rope_mla, with_ctx_out)
        x = x + g_m[:, None, :] * y
        x = x + g_f[:, None, :] * squared_relu_mlp(modulate(x, norm_mlp_w[layer], sh_f, sc_f),
                                                   mlp_w1[layer], mlp_w2[layer])
        if with_ctx_out:
            xc = xc + cg_m * yc
            xc = xc + cg_f * squared_relu_mlp(modulate(xc, norm_mlp_w[layer], csh_f, csc_f),
                                              mlp_w1[layer], mlp_w2[layer])
    return rms_norm(x, final_norm_w)


_drawn_inputs = setup_inputs


def setup_inputs(seed=0):
    import zlib

    import numpy as np

    out = dict(_drawn_inputs(seed))
    spreads = {}
    factors = {'norm_mix_w': 4.15,
     'gla_a_b': 2.808,
     'gla_norm_w': 8.0,
     'swa_sink': 8.0,
     'mla_q_norm_w': 8.0,
     'mla_kv_norm_w': 8.0,
     'norm_mlp_w': 2.764,
     'final_norm_w': 2.709}
    for name, (base, spread) in spreads.items():
        noise = np.random.default_rng([zlib.crc32(name.encode()), seed]).standard_normal(out[name].shape)
        drawn = base * np.exp(spread * noise) if base else spread * noise
        out[name] = __import__('jax').numpy.asarray(drawn.astype(out[name].dtype))
    for name, factor in factors.items():
        out[name] = (out[name] * factor).astype(out[name].dtype)
    return out
```

```python
from contextlib import ExitStack

import numpy as np

import concourse.bass as bass
from concourse import mybir

F32 = mybir.dt.float32
F32R = mybir.dt.float32r
U32 = mybir.dt.uint32
ALU = mybir.AluOpType
ACT = mybir.ActivationFunctionType
AX = mybir.AxisListType



class Step:

    def __init__(self, i, kind, layer, j=0, branch=0, q=0, h=0, heads=(), which=None, tn=0, tq=0, swa=False):
        self.i, self.kind, self.layer = i, kind, layer
        self.j, self.branch, self.q = j, branch, q
        self.h, self.heads, self.swa = h, heads, swa
        self.which, self.tn, self.tq = which, tn, tq
        self.block = None
        self.tiles, self.t, self.kc = 0, T, KC
        self.needs = self.after = -1
        self.pair, self.banks_of = 0, -1
        self.scores = None
        self.u, self.opens = 0, False
        self.a0 = 0


class Block:

    def __init__(self, name, layer, j, part, size, split):
        self.name, self.layer, self.j, self.part, self.size, self.split = name, layer, j, part, size, split
        self.first = self.last = None


P = 128
D = 1024
KC = D // P
NLAT = 256
T = 512
DEPTH = 2
EPS = 1e-6
GLA_HEADS, GLA_DK, GLA_DV, GLA_CHUNK, GLA_RANK = 4, 128, 256, 64, 16
NCH = T // GLA_CHUNK
HEAD = 128
SWA_SCALE = HEAD ** -0.5
MLA_SCALE = (128 + 64) ** -0.5
MLA_Q, MLA_KV = 384, 256
FF = 4 * D
QUARTER = FF // 4
NEG = -1e30
SLOT = KC * 2 * P
NRAW = 2
NSPLIT = 2
AHEAD = 2
NP_SWA = 3

OFF = dict(zip(("gq", "gk", "gv", "gr", "gzf", "gzb", "sq", "sk", "sv", "cq", "ckv", "kr", "gates"),
               np.cumsum([0, 512, 512, 1024, 1024, 16, 16, 1024, 256, 256, 384, 256, 64]).tolist()))

CONST = {}
_at = 0
for _name, _n in (("ident", P), ("ones", P), ("tri", 2 * P), ("band", 2 * P), ("swa_cos", NLAT),
                  ("swa_sin", NLAT), ("mla_cos", NLAT), ("mla_sin", NLAT)):
    CONST[_name] = slice(_at, _at + _n)
    _at += _n
NCONST = _at

VEC = {}
_at = 0
for _l in range(DEPTH):
    for _name, _n in (("mix", KC), ("mlp", KC), ("ada_b", 6 * KC), ("gla", 2), ("mq", 3), ("mkv", 2), ("sink", 8)):
        VEC[_name, _l] = slice(_at, _at + _n)
        _at += _n
VEC["final", 0] = slice(_at, _at + KC)
NVEC = _at + KC

GEMMS = ("zk", "gq", "gk", "gv", "gr", "sq", "sk", "sv", "cq", "ukn", "uv", "uqn", "uqp",
         "gate", "branch", "out", "up", "down")


def plan():
    steps, blocks = [], []
    last_stage = [-1]

    def add(kind, **kw):
        s = Step(len(steps), kind, **kw)
        s.after = max(last_stage[0], s.i - 2)
        steps.append(s)
        return s

    def stage(kind, **kw):
        s = add(kind, **kw)
        last_stage[0] = s.i
        return s

    def block(name, layer, j, part, size, split=True):
        blocks.append(Block(name, layer, j, part, size, split))
        return len(blocks) - 1

    def fill(calls, n):
        for _ in range(n):
            next(calls, lambda: None)()

    def gemm(kind, l, j, t=T, size=SLOT, tiles=2, old=None, kc=KC, needs=-1, a0=0, **kw):
        s = add(kind, layer=l, j=j, **kw)
        s.block = block(kind, l, j, kw.get("branch", kw.get("q", 0)), size) if old is None else old
        s.t, s.tiles, s.kc, s.needs, s.a0 = t, tiles, kc, needs, a0
        b = blocks[s.block]
        b.first = s.i if b.first is None else b.first
        b.last = s.i
        return s

    ada = [0]

    def modulation(l, j, first=False):
        s = add("ada", layer=l, j=j)
        s.u, s.opens, s.after = ada[0], first, last_stage[0]
        ada[0] += 1
        s.block = block("ada", l, j, 0, SLOT, split=False)
        blocks[s.block].first = blocks[s.block].last = s.i

    def modulations(l, blocks_of_l):
        for j in blocks_of_l:
            yield lambda j=j: modulation(l, j, j == blocks_of_l[0])

    for j in range(8):
        modulation(0, j, j == 0)
    stage("mod", layer=0, q=0).u = 7
    extra = modulations(0, range(8, 24))
    for l in range(DEPTH):
        tq = T if l < DEPTH - 1 else NLAT
        norm = stage("norm", layer=l, which="mix", tn=T)
        gemm("zk", l, 0, needs=norm.i)
        gemm("gq", l, 0, t=tq)
        gemm("gk", l, 0)
        before, done = steps[-1].i, None
        for h in range(GLA_HEADS):
            first = stage("gla1", layer=l, h=h, tq=tq)
            first.needs = before
            if done:
                fifth = stage("gla5", layer=l, h=h - 1, tq=tq)
                fifth.needs = done.i
            gate = gemm("gr", l, h, t=tq, tiles=1)
            second = stage("gla2", layer=l, h=h, tq=tq)
            second.needs = fifth.i if done else first.i
            v = gemm("gv", l, h, tiles=1)
            gemm("gv", l, h, tiles=1, old=v.block, a0=1)
            third = stage("gla3", layer=l, h=h, tq=tq)
            third.needs = second.i
            gemm("gr", l, h, t=tq, tiles=1, old=gate.block, a0=1)
            done = stage("gla4", layer=l, h=h, tq=tq)
            done.needs = third.i
            before = done.i
            if h == 1:
                gemm("gq", l, 1, t=tq)
                gemm("gk", l, 1)
        gemm("gate", l, 0, t=tq, branch=0)
        mixed = stage("gla5", layer=l, h=GLA_HEADS - 1, tq=tq)
        mixed.needs = done.i

        def branches(b, mixed):
            for j in range(4):
                if b or j:
                    gemm("gate", l, j, t=tq, branch=b)
                    fill(extra, 1)
                gemm("branch", l, j, t=tq, branch=b, needs=mixed.i if j == 0 else -1)
                fill(extra, 1)

        branches(0, mixed)
        keys = gemm("sk", l, 0)
        keys.after = keys.i - 1
        fill(extra, 1)
        rope = keys
        for p in range(4):
            query = gemm("sq", l, p, t=tq)
            query.after = max(query.after, rope.i)
            rope = query
            fill(extra, 1)
        gemm("sv", l, 0)
        mixed = stage("attn", layer=l, heads=range(8), tq=tq, swa=True)
        branches(1, mixed)
        if l == 0:
            stage("mod", layer=0, q=1).u = 23
        gemm("cq", l, 0, t=tq)
        gemm("cq", l, 1)
        gemm("cq", l, 2, t=tq, size=SLOT // 2, tiles=1)
        latent = stage("cnorm", layer=l, tq=tq)
        for p in range(4):
            s = gemm("uqn", l, p, size=3 * 384, kc=3, t=tq, needs=latent.i if p == 0 else -1)
            gemm("uqp", l, p, kc=3, t=tq, tiles=1, old=s.block)
            s = gemm("uv", l, p, size=2 * 512, kc=2)
            gemm("ukn", l, p, kc=2, old=s.block)
            mixed = stage("attn", layer=l, heads=range(2 * p, 2 * p + 2), tq=tq, swa=False)
        branches(2, mixed)
        merged = stage("merge", layer=l, tq=tq)
        for j in range(4):
            gemm("out", l, j, t=tq, needs=merged.i if j == 0 else -1)
        norm = stage("norm", layer=l, which="mlp", tn=tq)
        extra = modulations(l + 1, range(24) if l + 1 < DEPTH else ())
        up = {}
        down = {}
        for q, kind in ((0, "up"), (1, "up"), (0, "down"), (2, "up"), (1, "down"), (3, "up"), (2, "down"), (3, "down")):
            for j in range(4):
                if kind == "up":
                    s = gemm("up", l, j, t=tq, q=q, needs=norm.i if (q, j) == (0, 0) else -1)
                    if q >= 2:
                        s.after = max(s.after, down[q - 2].i)
                    up[q] = s
                else:
                    down[q] = gemm("down", l, j, t=tq, q=q, needs=up[q].i if j == 0 else -1)
                fill(extra, 1)
        if l + 1 < DEPTH:
            stage("mod", layer=l + 1, q=2).u = 47
    stage("norm", layer=0, which="final", tn=NLAT)
    products = [s for s in steps if s.kind in GEMMS]
    for n, s in enumerate(products):
        s.pair = n % 2
        s.banks_of = products[n - 2].i if n >= 2 else -1
        s.scores = next((a for a in steps[:s.i] if a.kind == "attn" and a.i > s.banks_of), None)
    return steps, blocks


def runs(blocks):
    out = []
    for b in blocks:
        if out and out[-1][0] == b.size:
            out[-1][1] += 1
        else:
            out.append([b.size, 1])
    return out


def counts(s):
    k = s.kind
    nq = s.tq // P
    if k == "ada":
        return dict(pe=[("mod_columns", 1)] * (not s.opens), act=[("mod_copied", 1)],
                    dve=[("mod_reduced", 1)] * (not s.opens))
    if k == "mod":
        return dict(pe=[("mod_columns", 1)], dve=[("mod_reduced", 1), ("mod_final", (2, 2, 3)[s.q])])
    if k == "norm":
        fin = s.which == "final"
        return dict(pe=[("norm_sum", 1)], act=[("norm_squares", 1), ("norm_root", 1)] + ([] if fin else [("norm_shifted", KC), ("norm_high", KC)]),
                    dve=[("norm_reduced", 1), ("norm_inverse", 1), ("norm_scaled", KC)] + ([] if fin else [("norm_low", KC)]))
    if k == "gla1":
        return dict(pe=[("gla_z", 2)], act=[("gla_abs", 2), ("gla_exp_z", 2), ("gla_ln", 2)], dve=[("gla_la", 2)],
                    pool=[("gla_zeroed", 2)] if s.h == 0 else [])
    if k == "gla2":
        return dict(pe=[("gla_sums", 2)], act=[("gla_exps", 4), ("gla_exp_end", 2)],
                    dve=[("gla_last", 2), ("gla_to_end", 2), ("gla_kinv", 2)], pool=[("gla_qdec", 2), ("gla_kend", 2)])
    if k == "gla3":
        return dict(pe=[("gla_kend_t", 2), ("gla_a", 2)], act=[("gla_kend_s", 4)], dve=[("gla_masked", 2)])
    if k == "gla4":
        return dict(pe=[("gla_u", NCH - 1), ("gla_o", 1)], act=[("gla_sumsq", nq), ("gla_root", 1)],
                    dve=[("gla_state", 2 * (NCH - 1)), ("gla_inverse", 1), ("gla_o_s", nq)])
    if k == "gla5":
        return dict(pe=[("gla_o_t", 1)], act=[("gla_high", 2)], dve=[("gla_out", 2), ("gla_low", 2)])
    if k == "attn":
        n = len(s.heads) * nq
        masked = [("att_masked", 2 * len(s.heads)), ("att_sunk", n), ("att_total", n)] if s.swa else []
        return dict(pe=[("att_scores", n), ("att_p_t", n), ("att_pv", n)],
                    act=[("att_exp", n)] + [("att_exp_sink", n)] * s.swa + [("att_p_s", n), ("att_o_s", len(s.heads)), ("att_high", len(s.heads))],
                    dve=masked + [("att_max", n), ("att_inverse", n), ("att_p", n), ("att_low", len(s.heads))])
    if k == "cnorm":
        return dict(pe=[("lat_sum", 2)], act=[("lat_squares", 2), ("lat_root", 2), ("lat_kr", 2), ("lat_high", 5)],
                    dve=[("lat_reduced", 2), ("lat_inverse", 2), ("lat_rope", 3), ("lat_scaled", 5), ("lat_low", 5)],
                    pool=[("lat_zeroed", 2), ("lat_k_roped", 2)])
    if k == "merge":
        return dict(act=[("merge_high", KC)], dve=[("merge_low", KC)])
    e = dict(pe=[("product", s.tiles)])
    ctx = s.t > NLAT
    if k == "gv":
        e.update(dict(dve=[("dve_evac", 1)]) if s.a0 else dict(act=[("act_evac", 1)]))
    elif k in ("zk", "gq", "gk", "sv", "ukn", "uv", "uqn"):
        e.update(act=[("act_evac", 1)], dve=[("dve_evac", 1)])
    elif k == "cq":
        e.update(act=[("act_evac", 1)], **(dict(dve=[("dve_evac", 1)]) if s.tiles > 1 else {}))
    elif k == "gr":
        e.update(act=[("act_evac", 1)])
    elif k in ("sq", "sk"):
        e.update(dve=[("dve_rope", 5)], pool=[("pool_evac", 1)], **(dict(act=[("act_evac", 1)]) if ctx else {}))
    elif k == "uqp":
        e.update(dve=[("dve_rope", 3)], pool=[("pool_evac", 1)], **(dict(act=[("act_evac", 1)]) if ctx else {}))
    elif k == "gate":
        e.update(act=[("act_evac", 2)])
    elif k == "branch":
        e.update(dve=[("dve_evac", 1)], **(dict(pool=[("pool_evac", 1)]) if s.branch else {}))
    elif k == "up":
        e.update(act=[("act_evac", 1), ("up_high", 1)], pool=[("pool_evac", 1)], dve=[("up_low", 1)])
    else:
        e.update(dve=[("dve_evac", 2 * (s.t // NLAT))])
    return e


def build(nc, xt, cvec, consts, vectors, decay_w, weights, out):
    steps, blocks = plan()
    ENGINES = ("pe", "act", "dve", "pool")

    before, ends, running = [], {e: [] for e in ENGINES}, {}
    last = {e: None for e in ENGINES}
    for s in steps:
        before.append(dict(running))
        for e, names in counts(s).items():
            for name, n in names:
                running[name] = running.get(name, 0) + n
            if names:
                last[e] = (names[-1][0], running[names[-1][0]])
        for e in ENGINES:
            ends[e].append(last[e])

    def value(name, s, n):
        return before[s.i].get(name, 0) + n

    def finished(engine, i):
        name, count = (ends[engine][i] if i >= 0 else None) or ("consts_in", 48)
        return sems[name], count

    split_of = {}
    for b in blocks:
        if b.split:
            split_of[id(b)] = len(split_of)
    split_blocks = [b for b in blocks if b.split]

    def room_for(n, s):
        m = blocks.index(split_blocks[n]) - NRAW
        return (n < NSPLIT or split_blocks[n - NSPLIT].last < s.i) and (m < 0 or blocks[m].split or blocks[m].last < s.i)

    with ExitStack() as ctx:
        top = [(nc.sbuf_base + 63) // 64 * 64]

        def fixed(name, shape, dt=F32):
            n = 4 * int(np.prod(shape[1:]))
            t = nc.alloc_sbuf_tensor_at(name, shape, dt, offset=top[0])
            top[0] += (n + 63) // 64 * 64
            return t

        x = fixed("x", [P, KC, T])
        hsplit = fixed("hsplit", [P, 2, KC, T], F32R)
        o_base = top[0]
        osplit = fixed("osplit", [P, 2, KC, T], F32R)
        wsplit = fixed("wsplit", [P, NSPLIT, 2, SLOT], F32R)
        raw = fixed("raw", [P, NRAW, SLOT])
        cst = fixed("cst", [P, NCONST])
        vec = fixed("vec", [P, NVEC])
        dw_base = top[0]
        dw = fixed("dw", [P, 2, 512])
        zt = fixed("zt", [P, T])
        kr = fixed("kr", [P, T])
        cs = fixed("cs", [P, KC, 32])
        part_base = top[0]
        part = fixed("part", [P, 2, 256])
        mod = fixed("mod", [P, DEPTH, 6 * KC, 2])
        gain = fixed("gain", [P, DEPTH, 2, KC, 2])
        nsink = fixed("nsink", [P, DEPTH, 8])
        tiny = fixed("tiny", [P, 1])
        stats = fixed("stats", [P, 6, 32])
        mg_base = top[0]
        mg = fixed("mg", [P, KC, T])
        scratch = top[0]
        end = nc.sbuf_usable_end

        def region(base, **shapes):
            got, at = {}, base
            for name, shape in shapes.items():
                dt = F32R if name.endswith("_r") else F32
                got[name] = nc.alloc_sbuf_tensor_at(name, [P, *shape], dt, offset=at)
                at += (4 * int(np.prod(shape)) + 63) // 64 * 64
            assert at <= end, (sorted(shapes), at, end)
            return got

        nrm = region(mg_base, xn=(KC, T), root=(T,), rinv=(T,))
        gla = region(mg_base, gq_s=(2, T), gk_s=(2, T), gv_s=(4, 256), gr_s=(2, T), la=(2, T), ep=(2, T),
                     en=(2, T), ke=(2, T), qd=(2, T), ktp=(2, 4, 2, P), at=(2, T), st=(2, 2, 256), last=(2, NCH))
        br = region(scratch, sg=(2, 2, T), bt=(2, 2, T))
        swa = region(scratch, sk_s=(2, T), sv_s=(4, 256), sq_s=(8, T), rp=(2, 2, NLAT), swa_p=(NP_SWA, T), swa_pt=(2, T), swa_o=(T,))
        mla = region(scratch, cn_r=(2, 5, T), kn=(2, T), vm=(4, 256), qn=(2, T), qp=(T,), mla_p=(2, T), mla_pt=(T,), mla_pt2=(T,))
        lat = region(scratch + 4 * 2 * 5 * T, cx=(5, T), cx_sq=(5, T))
        lat_sum = nc.alloc_sbuf_tensor_at("lat_sum", [P, 2, T], F32, offset=o_base)
        kpe = nc.alloc_sbuf_tensor_at("kpe", [P, 2, T], F32, offset=dw_base)
        mla_o = nc.alloc_sbuf_tensor_at("mla_o", [P, T], F32, offset=part_base)
        hid = [nc.alloc_sbuf_tensor_at("hid0", [P, 2, KC, T], F32R, offset=o_base),
               nc.alloc_sbuf_tensor_at("hid1", [P, 2, KC, T], F32R, offset=mg_base)]
        ups = region(mg_base + 4 * 2 * KC * T, rt=(2, 2, T))

        swa_probs = [swa["swa_p"][:, n, :] for n in range(NP_SWA)]
        mla_probs = [mla["mla_p"][:, 0, :], mla["mla_p"][:, 1, :], kr[:, :]]
        mla_turned = [mla["mla_pt"][:, :], mla["mla_pt2"][:, :]]

        o_s = gla["qd"][:, :, :].rearrange("p a (b n) -> p (a b) n", n=256)

        psum_g = nc.alloc_psum_tensor("psum_g", [P, 4, T], F32)
        psum_w = nc.alloc_psum_tensor("psum_w", [P, 4, T], F32)

        sems = {}
        for name in sorted(running) + ["w_high", "consts_in", "x_in", "dw_in", "zt_ready", "init_act", "init_dve", "out_done"]:
            sems[name] = ctx.enter_context(nc.semaphore(name))
        raw_in = [ctx.enter_context(nc.semaphore(f"raw_in{n}")) for n in range(NRAW)]
        raw_used = [ctx.enter_context(nc.semaphore(f"raw_used{n}")) for n in range(NRAW)]

        C = {n: cst[:, s] for n, s in CONST.items()}

        def chunk_cols(c):
            return slice(c * GLA_CHUNK, (c + 1) * GLA_CHUNK)

        half = T // GLA_CHUNK // 2
        ORDER = ([*range(half, NCH), *range(half)], [*reversed(range(half, NCH)), *reversed(range(half))])

        def last_col(d, c):
            return c * GLA_CHUNK + (GLA_CHUNK - 1 if d == 0 else 0)

        opening = 8

        block = ctx.enter_context(nc.Block())

        @block.sync
        def _(sp):
            sp.dma_start(cst[:], consts).then_inc(sems["consts_in"], 16)
            sp.dma_start(vec[:], vectors).then_inc(sems["consts_in"], 16)
            sp.dma_start(cs[:], cvec).then_inc(sems["consts_in"], 16)
            sp.dma_start(x[:], xt).then_inc(sems["x_in"], 16)

            n = at = 0
            for size, count in runs(blocks):
                stream = weights[at:at + count * P * size].rearrange("(u p n) -> u p n", p=P, n=size)
                at += count * P * size
                k = 0
                while k < count and (n % NRAW or n < NRAW):
                    if n >= NRAW:
                        sp.wait_ge(raw_used[n % NRAW], n // NRAW)
                    sp.dma_start(raw[:, n % NRAW, :size], stream[k]).then_inc(raw_in[n % NRAW], 16)
                    k, n = k + 1, n + 1
                pairs = (count - k) // NRAW
                if pairs > 1:
                    with sp.Fori(0, pairs) as i:
                        for r in range(NRAW):
                            sp.wait_ge(raw_used[r], i + n // NRAW)
                            sp.dma_start(raw[:, r, :size], stream[bass.ds(i * NRAW + (k + r), 1)]
                                         .rearrange("u p n -> p (u n)")).then_inc(raw_in[r], 16)
                    k, n = k + pairs * NRAW, n + pairs * NRAW
                while k < count:
                    sp.wait_ge(raw_used[n % NRAW], n // NRAW)
                    sp.dma_start(raw[:, n % NRAW, :size], stream[k]).then_inc(raw_in[n % NRAW], 16)
                    k, n = k + 1, n + 1
            for c in range(KC):
                sp.wait_ge(sems["norm_scaled"], value("norm_scaled", steps[-1], c + 1))
                sp.dma_start(out[:, c, :], nrm["xn"][:, c, 0:NLAT]).then_inc(sems["out_done"], 16)
            sp.wait_ge(sems["out_done"], 16 * KC)

        def arrived(n):
            return raw_in[n % NRAW], 16 * (n // NRAW + 1)

        def used(n):
            return raw_used[n % NRAW], n // NRAW + 1

        @block.tensor
        def _(pe):
            mm, tr = nc.tensor.matmul, nc.tensor.transpose
            g = [psum_g[:, b, :] for b in range(4)]
            w = [psum_w[:, b, :] for b in range(4)]

            def three(dst, a, b, first, final):
                mm(dst, a[0], b[0], start=first, stop=False, skip_group_check=True)
                mm(dst, a[0], b[1], start=False, stop=False, skip_group_check=True)
                return mm(dst, a[1], b[0], start=False, stop=final, skip_group_check=True)

            def product(s):
                b = blocks[s.block]
                n = split_of[id(b)]
                if b.first == s.i:
                    pe.wait_ge(*used(s.block))
                pe.wait_ge(*finished("act", s.banks_of))
                pe.wait_ge(*finished("dve", s.banks_of))
                if s.scores:
                    pe.wait_ge(sems["att_exp"], value("att_exp", s.scores, len(s.scores.heads) * s.scores.tq // P))
                if s.kind in ("down",):
                    act = hid[s.q % 2]
                elif s.kind == "branch":
                    act = osplit
                elif s.kind in ("ukn", "uv", "uqn", "uqp"):
                    act = mla["cn_r"]
                else:
                    act = hsplit
                if s.needs >= 0:
                    k = steps[s.needs].kind
                    if k not in ("norm", "merge"):
                        pe.wait_ge(*finished("act", s.needs))
                        pe.wait_ge(*finished("dve", s.needs))
                        pe.wait_ge(*finished("pool", s.needs))
                wide = b.size // s.kc
                wv = wsplit[:, n % NSPLIT, :, :b.size].rearrange("p h (k n) -> p h k n", n=wide)
                k0 = {"ukn": 3, "uv": 3}.get(s.kind, 0)
                col0 = {"uv": 256, "uqp": 256}.get(s.kind, 0)
                for a in range(s.a0, s.a0 + s.tiles):
                    bank = g[2 * s.pair + a - s.a0]
                    if s.kind in ("gv", "sv", "uv"):
                        for tt in (2 * a, 2 * a + 1):
                            dst = bank[:, (tt % 2) * 256:(tt % 2) * 256 + 256]
                            for k in range(s.kc):
                                hs = [act[:, i, k0 + k, tt * P:(tt + 1) * P] for i in (0, 1)]
                                ws = [wv[:, i, k, col0:col0 + 256] for i in (0, 1)]
                                ins = three(dst, hs, ws, k == 0, k == s.kc - 1)
                    else:
                        c0 = col0 + a * P
                        for k in range(s.kc):
                            if a == 0 and s.needs >= 0 and steps[s.needs].kind in ("norm", "merge"):
                                st = steps[s.needs]
                                if st.kind == "norm":
                                    pe.wait_ge(sems["norm_low"], value("norm_low", st, k + 1))
                                else:
                                    pe.wait_ge(sems["merge_low"], value("merge_low", st, k + 1))
                            ws = [wv[:, i, k, c0:c0 + P] for i in (0, 1)]
                            hs = [act[:, i, k0 + k, 0:s.t] for i in (0, 1)]
                            ins = three(bank[:, 0:s.t], ws, hs, k == 0, k == s.kc - 1)
                    ins.then_inc(sems["product"], 1)

            def mod_columns(s, u):
                pe.wait_ge(sems["mod_copied"], u + 1)
                if u >= 2:
                    pe.wait_ge(sems["mod_reduced"], u - 1)
                for i in range(2):
                    ins = tr(w[2 + u % 2][:, i * P:(i + 1) * P], part[:, u % 2, i * P:(i + 1) * P], C["ident"])
                ins.then_inc(sems["mod_columns"], 1)

            def ada(s):
                pe.wait_ge(*finished("act", s.after))
                pe.wait_ge(*finished("dve", s.after))
                pe.wait_ge(*arrived(s.block))
                if s.u >= 2:
                    pe.wait_ge(sems["mod_copied"], s.u - 1)
                rows = w[s.u % 2]
                for r in range(2):
                    for q in range(4):
                        k = 2 * q + r
                        ins = mm(rows[32 * q:32 * q + 32, 0:256], cs[:, k, :], raw[:, s.block % NRAW, k * 256:(k + 1) * 256],
                                 start=r == 0, stop=r == 1, skip_group_check=True)
                ins.then_inc(raw_used[s.block % NRAW], 1)
                if not s.opens:
                    mod_columns(s, s.u - 1)

            def gla_part(s):
                nq = s.tq // P
                cols = slice(s.h * P, (s.h + 1) * P)
                pe.wait_ge(*finished("act", s.needs))
                pe.wait_ge(*finished("dve", s.needs))
                pe.wait_ge(*finished("pool", s.needs))
                if s.kind == "gla1":
                    pe.wait_ge(sems["dw_in"], 16 * (s.layer + 1))
                    for d in range(2):
                        for tt in range(4):
                            ins = mm(w[d][:, tt * P:(tt + 1) * P], zt[:, tt * P:(tt + 1) * P], dw[:, d, cols], start=True, stop=True)
                        ins.then_inc(sems["gla_z"], 1)
                elif s.kind == "gla2":
                    for d in range(2):
                        for tt in range(4):
                            ins = mm(w[2 + d][:, tt * P:(tt + 1) * P], gla["la"][:, d, tt * P:(tt + 1) * P],
                                     C["tri"][:, d * P:(d + 1) * P], start=True, stop=True)
                        ins.then_inc(sems["gla_sums"], 1)
                elif s.kind == "gla3":
                    for d in range(2):
                        for tt in range(4):
                            ins = tr(w[d][:, tt * P:(tt + 1) * P], gla["ke"][:, d, tt * P:(tt + 1) * P], C["ident"])
                        ins.then_inc(sems["gla_kend_t"], 1)
                    for d in range(2):
                        for tt in range(nq):
                            c = slice(tt * P, (tt + 1) * P)
                            ins = mm(w[2 + d][:, c], gla["en"][:, d, c], gla["qd"][:, d, c], start=True, stop=True)
                        ins.then_inc(sems["gla_a"], 1)
                elif s.kind == "gla4":
                    for tt in range(nq):
                        for d in range(2):
                            mm(w[2 + tt // 2][:, (tt % 2) * 256:(tt % 2) * 256 + 256], gla["at"][:, d, tt * P:(tt + 1) * P],
                               gla["gv_s"][:, tt, :], start=(tt % 2 == 0 and d == 0), stop=False, skip_group_check=True)
                    for n in range(NCH):
                        if n < NCH - 1:
                            if n >= 2:
                                pe.wait_ge(sems["gla_state"], value("gla_state", s, 2 * (n - 1)))
                            for d in range(2):
                                c = ORDER[d][n]
                                ins = mm(w[n % 2][:, d * 256:(d + 1) * 256], gla["ktp"][:, d, c // 2, c % 2, :], gla["gv_s"][:, c // 2, :],
                                         start=True, stop=True)
                            ins.then_inc(sems["gla_u"], 1)
                        if n:
                            pe.wait_ge(sems["gla_state"], value("gla_state", s, 2 * n))
                            for d in range(2):
                                c = ORDER[d][n]
                                tt = c // 2
                                if tt < nq:
                                    ins = mm(w[2 + tt // 2][64 * (c % 2):64 * (c % 2) + 64, (tt % 2) * 256:(tt % 2) * 256 + 256],
                                             gla["qd"][:, d, chunk_cols(c)], gla["st"][:, d, n % 2, :], start=False,
                                             stop=(n == NCH - 1), skip_group_check=True)
                    ins.then_inc(sems["gla_o"], 1)
                else:
                    for c in range(2):
                        for tt in range(nq):
                            ins = tr(w[2 + c][:, tt * P:(tt + 1) * P], o_s[:, tt, c * P:(c + 1) * P], C["ident"])
                    ins.then_inc(sems["gla_o_t"], 1)

            def attention(s):
                nq = s.tq // P
                items = [(hd, qt) for hd in s.heads for qt in range(nq)]
                probs = swa_probs if s.swa else mla_probs
                pe.wait_ge(*finished("pe", s.i - 1))
                pe.wait_ge(*finished("act", s.i - 1))
                pe.wait_ge(*finished("dve", s.i - 1))
                pe.wait_ge(*finished("pool", s.i - 1))

                def scores(i):
                    hd, qt = items[i]
                    keys = slice(0, T) if qt < 2 else slice(NLAT, T)
                    qc = slice(qt * P, (qt + 1) * P)
                    if i >= 4:
                        pe.wait_ge(sems["att_exp"], value("att_exp", s, i - 3))
                    dst = g[i % 4][:, keys]
                    if s.swa:
                        ins = mm(dst, swa["sq_s"][:, hd, qc], swa["sk_s"][:, hd // 4, keys], start=True, stop=True)
                    else:
                        mm(dst, mla["qn"][:, hd % 2, qc], mla["kn"][:, hd % 2, keys], start=True, stop=False)
                        ins = mm(dst, mla["qp"][:, qc], kpe[:, hd % 2, keys], start=False, stop=True)
                    ins.then_inc(sems["att_scores"], 1)

                def transposed(i):
                    qt = items[i][1]
                    pe.wait_ge(sems["att_p"], value("att_p", s, i + 1))
                    if i >= 2:
                        pe.wait_ge(sems["att_p_s"], value("att_p_s", s, i - 1))
                    for kt in range(0 if qt < 2 else 2, 4):
                        ins = tr(w[i % 2][:, kt * P:(kt + 1) * P], probs[i % len(probs)][:, kt * P:(kt + 1) * P], C["ident"])
                    ins.then_inc(sems["att_p_t"], 1)

                def values(i):
                    hd, qt = items[i]
                    pe.wait_ge(sems["att_p_s"], value("att_p_s", s, i + 1))
                    if qt == 0 and i >= 2 * nq:
                        pe.wait_ge(sems["att_o_s"], value("att_o_s", s, i // nq - 1))
                    pt = swa["swa_pt"][:, i % 2, :] if s.swa else mla_turned[i % 2]
                    lo = 0 if qt < 2 else 2
                    for kt in range(lo, 4):
                        v = swa["sv_s"][:, kt, (hd // 4) * P:(hd // 4 + 1) * P] if s.swa else mla["vm"][:, kt, (hd % 2) * P:(hd % 2 + 1) * P]
                        ins = mm(w[2 + hd % 2][:, qt * P:(qt + 1) * P], v, pt[:, kt * P:(kt + 1) * P], start=kt == lo, stop=kt == 3)
                    ins.then_inc(sems["att_pv"], 1)

                n = len(items)
                for i in range(-AHEAD, n + 1):
                    if 0 <= i + AHEAD < n:
                        scores(i + AHEAD)
                    if 0 <= i < n:
                        transposed(i)
                    if i >= 1:
                        values(i - 1)

            pe.wait_ge(sems["consts_in"], 48)
            pe.wait_ge(sems["init_act"], 1)
            pe.wait_ge(sems["zt_ready"], 3)
            for s in steps:
                if s.kind in GEMMS:
                    product(s)
                elif s.kind == "ada":
                    ada(s)
                elif s.kind == "mod":
                    mod_columns(s, s.u)
                elif s.kind == "norm":
                    pe.wait_ge(*finished("pe", s.i - 1))
                    pe.wait_ge(*finished("act", s.i - 1))
                    pe.wait_ge(*finished("dve", s.i - 1))
                    pe.wait_ge(*finished("pool", s.i - 1))
                    pe.wait_ge(sems["norm_reduced"], value("norm_reduced", s, 1))
                    mm(w[0][:, :s.tn], C["ones"], nrm["rinv"][:, :s.tn], start=True, stop=True).then_inc(sems["norm_sum"], 1)
                elif s.kind == "cnorm":
                    pe.wait_ge(*finished("pe", s.i - 1))
                    pe.wait_ge(*finished("act", s.i - 1))
                    pe.wait_ge(*finished("dve", s.i - 1))
                    pe.wait_ge(*finished("pool", s.i - 1))
                    for i in range(2):
                        tn = s.tq if i == 0 else T
                        pe.wait_ge(sems["lat_reduced"], value("lat_reduced", s, i + 1))
                        mm(w[i][:, :tn], C["ones"], lat_sum[:, i, :tn], start=True, stop=True).then_inc(sems["lat_sum"], 1)
                elif s.kind[:3] == "gla":
                    gla_part(s)
                elif s.kind == "attn":
                    attention(s)

        @block.scalar
        def _(act):
            go = nc.scalar.activation
            split_next = [0]

            def round_weights(s, upto_block):
                while split_next[0] < min(upto_block + 2, len(split_blocks)) and room_for(split_next[0], s):
                    n = split_next[0]
                    b = split_blocks[n]
                    raw_n = blocks.index(b)
                    act.wait_ge(*arrived(raw_n))
                    if n >= NSPLIT:
                        act.wait_ge(*finished("pe", split_blocks[n - NSPLIT].last))
                    go(wsplit[:, n % NSPLIT, 0, :b.size], raw[:, raw_n % NRAW, :b.size], ACT.Copy).then_inc(sems["w_high"], 1)
                    split_next[0] += 1

            def evacuate(s):
                bank = [psum_g[:, 2 * s.pair + a, :] for a in range(2)]
                both = psum_g[:, 2 * s.pair:2 * s.pair + 2, :]
                names = dict(counts(s).get("act", []))
                if not names:
                    return
                act.wait_ge(*finished("act", s.i - 1))
                act.wait_ge(*finished("pe", s.after))
                act.wait_ge(*finished("dve", s.after))
                act.wait_ge(*finished("pool", s.after))
                k = s.kind
                if k in ("sq", "sk", "uqp"):
                    act.wait_ge(sems["dve_rope"], value("dve_rope", s, 5 if k != "uqp" else 2))
                    ctx_cols = slice(NLAT, T)
                    if k == "sq":
                        go(swa["sq_s"][:, 2 * s.j:2 * s.j + 2, ctx_cols], both[:, :, ctx_cols], ACT.Copy, scale=SWA_SCALE).then_inc(sems["act_evac"], 1)
                    elif k == "sk":
                        go(swa["sk_s"][:, :, ctx_cols], both[:, :, ctx_cols], ACT.Copy).then_inc(sems["act_evac"], 1)
                    else:
                        go(mla["qp"][:, ctx_cols], bank[0][:, ctx_cols], ACT.Copy, scale=MLA_SCALE).then_inc(sems["act_evac"], 1)
                    return
                act.wait_ge(sems["product"], value("product", s, 1))
                if k == "zk":
                    go(zt[0:32, :], bank[0][0:32, :], ACT.Copy).then_inc(sems["act_evac"], 1)
                elif k == "gq":
                    go(gla["gq_s"][:, 0, :s.t], bank[0][:, :s.t], ACT.Copy, scale=GLA_DK ** -0.5).then_inc(sems["act_evac"], 1)
                elif k == "gk":
                    go(gla["gk_s"][:, 0, :], bank[0], ACT.Copy).then_inc(sems["act_evac"], 1)
                elif k in ("gv", "sv", "uv"):
                    dst = {"gv": gla["gv_s"], "sv": swa["sv_s"], "uv": mla["vm"]}[k]
                    go(dst[:, 0:2, :], bank[0].rearrange("p (t n) -> p t n", n=256), ACT.Copy).then_inc(sems["act_evac"], 1)
                elif k == "gr":
                    go(gla["gr_s"][:, s.a0, :s.t], bank[0][:, :s.t], ACT.Silu).then_inc(sems["act_evac"], 1)
                elif k == "cq":
                    dst = lat["cx"][:, (0, 3, 2)[s.j], :s.t]
                    go(dst, bank[0][:, :s.t], ACT.Copy).then_inc(sems["act_evac"], 1)
                elif k == "ukn":
                    go(mla["kn"][:, 0, :], bank[0], ACT.Copy).then_inc(sems["act_evac"], 1)
                elif k == "uqn":
                    go(mla["qn"][:, 0, :s.t], bank[0][:, :s.t], ACT.Copy, scale=MLA_SCALE).then_inc(sems["act_evac"], 1)
                elif k == "gate":
                    for a in range(2):
                        act.wait_ge(sems["product"], value("product", s, a + 1))
                        go(br["sg"][:, s.j % 2, a, :s.t], bank[a][:, :s.t], ACT.Sigmoid).then_inc(sems["act_evac"], 1)
                elif k == "up":
                    act.wait_ge(sems["product"], value("product", s, 2))
                    go(ups["rt"][:, s.j % 2, :, :s.t], both[:, :, :s.t], ACT.Relu).then_inc(sems["act_evac"], 1)
                    act.wait_ge(sems["pool_evac"], value("pool_evac", s, 1))
                    go(hid[s.q % 2][:, 0, 2 * s.j:2 * s.j + 2, :s.t], ups["rt"][:, s.j % 2, :, :s.t], ACT.Copy).then_inc(sems["up_high"], 1)

            def gla_part(s):
                nq = s.tq // P
                act.wait_ge(*finished("act", s.i - 1))
                act.wait_ge(*finished("pe", s.needs))
                act.wait_ge(*finished("dve", s.needs))
                act.wait_ge(*finished("pool", s.needs))
                if s.kind == "gla1":
                    for d in range(2):
                        act.wait_ge(sems["gla_z"], value("gla_z", s, d + 1))
                        go(gla["la"][:, d, :], psum_w[:, d, :], ACT.Abs).then_inc(sems["gla_abs"], 1)
                        act.wait_ge(sems["gla_abs"], value("gla_abs", s, d + 1))
                        go(gla["la"][:, d, :], gla["la"][:, d, :], ACT.Exp, scale=-1.0).then_inc(sems["gla_exp_z"], 1)
                        act.wait_ge(sems["gla_exp_z"], value("gla_exp_z", s, d + 1))
                        go(gla["la"][:, d, :], gla["la"][:, d, :], ACT.Ln, bias=1.0).then_inc(sems["gla_ln"], 1)
                elif s.kind == "gla2":
                    for d in range(2):
                        act.wait_ge(sems["gla_sums"], value("gla_sums", s, d + 1))
                        go(gla["ep"][:, d, :], psum_w[:, 2 + d, :], ACT.Exp).then_inc(sems["gla_exps"], 1)
                        go(gla["en"][:, d, :], psum_w[:, 2 + d, :], ACT.Exp, scale=-1.0).then_inc(sems["gla_exps"], 1)
                    for d in range(2):
                        act.wait_ge(sems["gla_to_end"], value("gla_to_end", s, d + 1))
                        go(gla["ke"][:, d, :], gla["ke"][:, d, :], ACT.Exp).then_inc(sems["gla_exp_end"], 1)
                elif s.kind == "gla3":
                    for d in range(2):
                        act.wait_ge(sems["gla_kend_t"], value("gla_kend_t", s, d + 1))
                        for a in range(2):
                            rows = slice(64 * a, 64 * a + 64)
                            go(gla["ktp"][rows, d, :, a, :], psum_w[rows, d, :].rearrange("p (t n) -> p t n", n=P), ACT.Copy)\
                                .then_inc(sems["gla_kend_s"], 1)
                elif s.kind == "gla4":
                    act.wait_ge(sems["gla_o"], value("gla_o", s, 1))
                    for tt in range(nq):
                        src = psum_w[:, 2 + tt // 2, (tt % 2) * 256:(tt % 2) * 256 + 256]
                        go(gla["en"][:, tt // 2, (tt % 2) * 256:(tt % 2) * 256 + 256], src, ACT.Square,
                           accum_out=stats[:, 0, tt:tt + 1]).then_inc(sems["gla_sumsq"], 1)
                    act.wait_ge(sems["gla_sumsq"], value("gla_sumsq", s, nq))
                    go(stats[:, 1, 0:nq], stats[:, 0, 0:nq], ACT.Sqrt, scale=1.0 / GLA_DV, bias=tiny[:, 0:1]).then_inc(sems["gla_root"], 1)
                else:
                    for c in range(2):
                        act.wait_ge(sems["gla_out"], value("gla_out", s, c + 1))
                        go(osplit[:, 0, 2 * s.h + c, :s.tq], gla["ke"][:, c, :s.tq], ACT.Copy).then_inc(sems["gla_high"], 1)

            def attention(s):
                nq = s.tq // P
                n = len(s.heads) * nq
                probs = swa_probs if s.swa else mla_probs
                oc = swa["swa_o"] if s.swa else mla_o
                act.wait_ge(*finished("pe", s.i - 1))
                act.wait_ge(*finished("act", s.i - 1))
                act.wait_ge(*finished("dve", s.i - 1))
                act.wait_ge(*finished("pool", s.i - 1))

                def exponentials(i):
                    keys = slice(0, T) if i % nq < 2 else slice(NLAT, T)
                    if s.swa:
                        act.wait_ge(sems["att_sunk"], value("att_sunk", s, i + 1))
                    else:
                        act.wait_ge(sems["att_max"], value("att_max", s, i + 1))
                    if i >= len(probs):
                        act.wait_ge(sems["att_p_t"], value("att_p_t", s, i + 1 - len(probs)))
                    go(probs[i % len(probs)][:, keys], psum_g[:, i % 4, keys], ACT.Exp, bias=stats[:, 1 if s.swa else 0, i:i + 1],
                       accum_out=stats[:, 2, i:i + 1]).then_inc(sems["att_exp"], 1)
                    if s.swa:
                        hd = s.heads[i // nq]
                        go(stats[:, 3, i:i + 1], stats[:, 1, i:i + 1], ACT.Exp, bias=vec[:, VEC["sink", s.layer]][:, hd:hd + 1])\
                            .then_inc(sems["att_exp_sink"], 1)

                def copied(i):
                    keys = slice(0, T) if i % nq < 2 else slice(NLAT, T)
                    act.wait_ge(sems["att_p_t"], value("att_p_t", s, i + 1))
                    pt = swa["swa_pt"][:, i % 2, :] if s.swa else mla_turned[i % 2]
                    go(pt[:, keys], psum_w[:, i % 2, keys], ACT.Copy).then_inc(sems["att_p_s"], 1)

                def head_out(hh):
                    act.wait_ge(sems["att_pv"], value("att_pv", s, nq * (hh + 1)))
                    if hh:
                        act.wait_ge(sems["att_low"], value("att_low", s, hh))
                    go(oc[:, :s.tq], psum_w[:, 2 + hh % 2, :s.tq], ACT.Copy).then_inc(sems["att_o_s"], 1)
                    act.wait_ge(sems["att_o_s"], value("att_o_s", s, hh + 1))
                    go(osplit[:, 0, s.heads[hh], :s.tq], oc[:, :s.tq], ACT.Copy).then_inc(sems["att_high"], 1)

                for i in range(n + 1):
                    if i < n:
                        exponentials(i)
                    if i >= 1:
                        copied(i - 1)
                    if i > nq and i % nq == 1:
                        head_out(i // nq - 1)
                head_out(len(s.heads) - 1)

            act.wait_ge(sems["consts_in"], 48)
            go(cs[:], cs[:], ACT.Silu).then_inc(sems["init_act"], 1)
            act.wait_ge(sems["init_dve"], 1)
            next_split = -1
            for s in steps:
                if s.block is not None and blocks[s.block].split:
                    next_split = max(next_split, split_of[id(blocks[s.block])])
                round_weights(s, next_split if s.i > opening else -2)
                if s.kind in GEMMS:
                    evacuate(s)
                elif s.kind == "ada":
                    act.wait_ge(*finished("act", s.i - 1))
                    act.wait_ge(*used(s.block))
                    if s.u >= 2:
                        act.wait_ge(sems["mod_columns"], s.u - 1)
                    go(part[:, s.u % 2, :], psum_w[:, s.u % 2, 0:256], ACT.Copy).then_inc(sems["mod_copied"], 1)
                elif s.kind == "norm":
                    act.wait_ge(*finished("pe", s.i - 1))
                    act.wait_ge(*finished("act", s.i - 1))
                    act.wait_ge(*finished("dve", s.i - 1))
                    act.wait_ge(*finished("pool", s.i - 1))
                    if s.which == "mix":
                        act.dma_start(dw[:], decay_w[s.layer]).then_inc(sems["dw_in"], 16)
                        if s.layer == 0:
                            act.wait_ge(sems["x_in"], 16)
                    go(nrm["xn"][:, :, :s.tn], x[:, :, :s.tn], ACT.Square).then_inc(sems["norm_squares"], 1)
                    act.wait_ge(sems["norm_sum"], value("norm_sum", s, 1))
                    go(nrm["root"][:, :s.tn], psum_w[:, 0, :s.tn], ACT.Sqrt, scale=1.0 / D, bias=tiny[:, 0:1]).then_inc(sems["norm_root"], 1)
                    if s.which != "final":
                        m = {"mix": 0, "mlp": 1}[s.which]
                        for c in range(KC):
                            act.wait_ge(sems["norm_scaled"], value("norm_scaled", s, c + 1))
                            for r in range(s.tn // NLAT):
                                cols = slice(r * NLAT, (r + 1) * NLAT)
                                ins = go(nrm["xn"][:, c, cols], nrm["xn"][:, c, cols], ACT.Identity, scale=gain[:, s.layer, m, c, r:r + 1],
                                         bias=mod[:, s.layer, 3 * KC * m + c, r:r + 1])
                            ins.then_inc(sems["norm_shifted"], 1)
                            act.wait_ge(sems["norm_shifted"], value("norm_shifted", s, c + 1))
                            go(hsplit[:, 0, c, :s.tn], nrm["xn"][:, c, :s.tn], ACT.Copy).then_inc(sems["norm_high"], 1)
                elif s.kind == "cnorm":
                    act.wait_ge(*finished("pe", s.i - 1))
                    act.wait_ge(*finished("act", s.i - 1))
                    act.wait_ge(*finished("dve", s.i - 1))
                    act.wait_ge(*finished("pool", s.i - 1))
                    groups = ((0, 3, s.tq), (3, 5, T))
                    for a, b, tn in groups:
                        go(lat["cx_sq"][:, a:b, :tn], lat["cx"][:, a:b, :tn], ACT.Square).then_inc(sems["lat_squares"], 1)
                    for i, (a, b, tn) in enumerate(groups):
                        act.wait_ge(sems["lat_sum"], value("lat_sum", s, i + 1))
                        go(lat["cx_sq"][:, i, :tn], psum_w[:, i, :tn], ACT.Sqrt, scale=1.0 / (P * (b - a)), bias=tiny[:, 0:1]).then_inc(sems["lat_root"], 1)
                    for a in range(2):
                        rows = slice(64 * a, 64 * a + 64)
                        go(kpe[rows, a, NLAT:T], kr[rows, NLAT:T], ACT.Copy).then_inc(sems["lat_kr"], 1)
                    for c in range(5):
                        tn = s.tq if c < 3 else T
                        act.wait_ge(sems["lat_scaled"], value("lat_scaled", s, c + 1))
                        go(mla["cn_r"][:, 0, c, :tn], lat["cx"][:, c, :tn], ACT.Copy).then_inc(sems["lat_high"], 1)
                elif s.kind == "merge":
                    act.wait_ge(*finished("pe", s.i - 1))
                    act.wait_ge(*finished("act", s.i - 1))
                    act.wait_ge(*finished("dve", s.i - 1))
                    act.wait_ge(*finished("pool", s.i - 1))
                    for c in range(KC):
                        go(hsplit[:, 0, c, :s.tq], mg[:, c, :s.tq], ACT.Copy).then_inc(sems["merge_high"], 1)
                elif s.kind[:3] == "gla":
                    gla_part(s)
                elif s.kind == "attn":
                    attention(s)

        @block.vector
        def _(dve):
            v = nc.vector
            split_next = [0]

            def split_weights(s, upto_block):
                while split_next[0] < min(upto_block + 2, len(split_blocks)) and room_for(split_next[0], s):
                    n = split_next[0]
                    b = split_blocks[n]
                    raw_n = blocks.index(b)
                    dve.wait_ge(sems["w_high"], n + 1)
                    v.tensor_tensor(wsplit[:, n % NSPLIT, 1, :b.size], raw[:, raw_n % NRAW, :b.size],
                                    wsplit[:, n % NSPLIT, 0, :b.size].bitcast(F32), ALU.subtract).then_inc(raw_used[raw_n % NRAW], 1)
                    split_next[0] += 1

            def rope(s):
                both = psum_g[:, 2 * s.pair:2 * s.pair + 2, 0:NLAT]
                scale = SWA_SCALE if s.kind == "sq" else 1.0
                dve.wait_ge(sems["product"], value("product", s, 2))
                cos = C["swa_cos"].unsqueeze(1).broadcast_to([P, 2, NLAT])
                v.scalar_tensor_tensor(swa["rp"][:, 0], both, scale, cos, ALU.mult, ALU.mult).then_inc(sems["dve_rope"], 1)
                for a in range(4):
                    b = a ^ 1
                    src, dst = slice(32 * b, 32 * b + 32), slice(32 * a, 32 * a + 32)
                    sin = cst[src, CONST["swa_sin"]].unsqueeze(1).broadcast_to([32, 2, NLAT])
                    v.scalar_tensor_tensor(swa["rp"][dst, 1], psum_g[src, 2 * s.pair:2 * s.pair + 2, 0:NLAT], scale, sin,
                                           ALU.mult, ALU.mult).then_inc(sems["dve_rope"], 1)

            def evacuate(s):
                bank = [psum_g[:, 2 * s.pair + a, :] for a in range(2)]
                both = psum_g[:, 2 * s.pair:2 * s.pair + 2, :]
                if "dve" not in counts(s):
                    return
                dve.wait_ge(*finished("dve", s.i - 1))
                dve.wait_ge(*finished("pe", s.after))
                dve.wait_ge(*finished("act", s.after))
                dve.wait_ge(*finished("pool", s.after))
                k = s.kind
                if k in ("sq", "sk"):
                    rope(s)
                    return
                if k == "uqp":
                    dve.wait_ge(sems["product"], value("product", s, 1))
                    v.scalar_tensor_tensor(mla["mla_p"][:, 0, 0:NLAT], bank[0][:, 0:NLAT], MLA_SCALE, C["mla_cos"], ALU.mult, ALU.mult).then_inc(sems["dve_rope"], 1)
                    v.stream_shuffle(mla["mla_p"][:, 1, 0:NLAT], bank[0][:, 0:NLAT], [(r + 16) % 32 for r in range(32)]).then_inc(sems["dve_rope"], 1)
                    dve.wait_ge(sems["dve_rope"], value("dve_rope", s, 2))
                    v.scalar_tensor_tensor(mla["mla_p"][:, 1, 0:NLAT], mla["mla_p"][:, 1, 0:NLAT], MLA_SCALE, C["mla_sin"], ALU.mult, ALU.mult).then_inc(sems["dve_rope"], 1)
                    return
                dve.wait_ge(sems["product"], value("product", s, s.tiles))
                if k == "zk":
                    v.tensor_copy(kr[:], bank[1]).then_inc(sems["dve_evac"], 1)
                elif k == "gq":
                    v.tensor_scalar(gla["gq_s"][:, 1, :s.t], bank[1][:, :s.t], GLA_DK ** -0.5, None, ALU.mult).then_inc(sems["dve_evac"], 1)
                elif k == "gk":
                    v.tensor_copy(gla["gk_s"][:, 1, :], bank[1]).then_inc(sems["dve_evac"], 1)
                elif k in ("gv", "sv", "uv"):
                    dst = {"gv": gla["gv_s"], "sv": swa["sv_s"], "uv": mla["vm"]}[k]
                    v.tensor_copy(dst[:, 2:4, :], bank[s.tiles - 1].rearrange("p (t n) -> p t n", n=256)).then_inc(sems["dve_evac"], 1)
                elif k == "cq":
                    v.tensor_copy(lat["cx"][:, (1, 4)[s.j], :s.t], bank[1][:, :s.t]).then_inc(sems["dve_evac"], 1)
                elif k == "ukn":
                    v.tensor_copy(mla["kn"][:, 1, :], bank[1]).then_inc(sems["dve_evac"], 1)
                elif k == "uqn":
                    v.tensor_scalar(mla["qn"][:, 1, :s.t], bank[1][:, :s.t], MLA_SCALE, None, ALU.mult).then_inc(sems["dve_evac"], 1)
                elif k == "branch":
                    dve.wait_ge(*finished("act", s.i - 1))
                    dst = mg[:, 2 * s.j:2 * s.j + 2, :s.t] if s.branch == 0 else br["bt"][:, s.j % 2, :, :s.t]
                    v.tensor_tensor(dst, both[:, :, :s.t], br["sg"][:, s.j % 2, :, :s.t], ALU.mult).then_inc(sems["dve_evac"], 1)
                elif k == "up":
                    dve.wait_ge(sems["up_high"], value("up_high", s, 1))
                    v.tensor_tensor(hid[s.q % 2][:, 1, 2 * s.j:2 * s.j + 2, :s.t], ups["rt"][:, s.j % 2, :, :s.t],
                                    hid[s.q % 2][:, 0, 2 * s.j:2 * s.j + 2, :s.t].bitcast(F32), ALU.subtract).then_inc(sems["up_low"], 1)
                else:
                    m = 2 if k == "out" else 5
                    for a in range(2):
                        for r in range(s.t // NLAT):
                            c, cols = 2 * s.j + a, slice(r * NLAT, (r + 1) * NLAT)
                            v.scalar_tensor_tensor(x[:, c, cols], bank[a][:, cols], mod[:, s.layer, m * KC + c, r:r + 1], x[:, c, cols],
                                                   ALU.mult, ALU.add).then_inc(sems["dve_evac"], 1)

            def reduce_columns(s, u):
                dve.wait_ge(*finished("dve", s.i - 1))
                dve.wait_ge(sems["mod_columns"], value("mod_columns", s, 1))
                l, j = u // 24, u % 24
                src = psum_w[:, 2 + u % 2, 0:256].rearrange("p (t q n) -> p t n q", t=2, q=4)[:, :, 0:2, :]
                v.tensor_reduce(mod[:, l, 2 * j:2 * j + 2, :], src, AX.X, ALU.add).then_inc(sems["mod_reduced"], 1)

            def gla_part(s):
                nq = s.tq // P
                h2 = s.h % 2
                dve.wait_ge(*finished("dve", s.i - 1))
                dve.wait_ge(*finished("pe", s.needs))
                dve.wait_ge(*finished("act", s.needs))
                dve.wait_ge(*finished("pool", s.needs))
                if s.kind == "gla1":
                    for d in range(2):
                        dve.wait_ge(sems["gla_ln"], value("gla_ln", s, d + 1))
                        v.scalar_tensor_tensor(gla["la"][:, d, :], psum_w[:, d, :], 0.0, gla["la"][:, d, :], ALU.min, ALU.subtract)\
                            .then_inc(sems["gla_la"], 1)
                elif s.kind == "gla2":
                    for d in range(2):
                        dve.wait_ge(sems["gla_exps"], value("gla_exps", s, 2 * (d + 1)))
                        sums = psum_w[:, 2 + d, :].rearrange("p (c n) -> p c n", n=GLA_CHUNK)
                        v.tensor_copy(gla["last"][:, d, :], sums[:, :, last_col(d, 0)]).then_inc(sems["gla_last"], 1)
                        dve.wait_ge(sems["gla_last"], value("gla_last", s, d + 1))
                        v.tensor_tensor(gla["ke"][:, d, :].rearrange("p (c n) -> p c n", n=GLA_CHUNK),
                                        gla["last"][:, d, :].unsqueeze(2).broadcast_to([P, NCH, GLA_CHUNK]), sums, ALU.subtract)\
                            .then_inc(sems["gla_to_end"], 1)
                    for d in range(2):
                        v.tensor_tensor(gla["en"][:, d, :], gla["gk_s"][:, h2, :], gla["en"][:, d, :], ALU.mult).then_inc(sems["gla_kinv"], 1)
                elif s.kind == "gla3":
                    for d in range(2):
                        dve.wait_ge(sems["gla_a"], value("gla_a", s, d + 1))
                        mask = C["tri"][:, d * P:(d + 1) * P].bitcast(U32).unsqueeze(1).broadcast_to([P, nq, P])
                        v.copy_predicated(gla["at"][:, d, :s.tq].rearrange("p (t n) -> p t n", n=P), mask,
                                          psum_w[:, 2 + d, :s.tq].rearrange("p (t n) -> p t n", n=P)).then_inc(sems["gla_masked"], 1)
                elif s.kind == "gla4":
                    for n in range(NCH - 1):
                        dve.wait_ge(sems["gla_u"], value("gla_u", s, n + 1))
                        for d in range(2):
                            c = ORDER[d][n]
                            u = psum_w[:, n % 2, d * 256:(d + 1) * 256]
                            if n == 0:
                                v.tensor_copy(gla["st"][:, d, 1, :], u).then_inc(sems["gla_state"], 1)
                            else:
                                dve.wait_ge(sems["gla_state"], value("gla_state", s, 2 * n - 1 + d))
                                v.scalar_tensor_tensor(gla["st"][:, d, (n + 1) % 2, :], gla["st"][:, d, n % 2, :],
                                                       gla["ep"][:, d, last_col(d, c):last_col(d, c) + 1], u, ALU.mult, ALU.add)\
                                    .then_inc(sems["gla_state"], 1)
                    dve.wait_ge(sems["gla_root"], value("gla_root", s, 1))
                    v.reciprocal(stats[:, 2, 0:nq], stats[:, 1, 0:nq]).then_inc(sems["gla_inverse"], 1)
                    dve.wait_ge(sems["gla_inverse"], value("gla_inverse", s, 1))
                    for tt in range(nq):
                        v.tensor_scalar(o_s[:, tt, :], psum_w[:, 2 + tt // 2, (tt % 2) * 256:(tt % 2) * 256 + 256],
                                        stats[:, 2, tt:tt + 1], None, ALU.mult).then_inc(sems["gla_o_s"], 1)
                else:
                    dve.wait_ge(sems["gla_o_t"], value("gla_o_t", s, 1))
                    for c in range(2):
                        v.scalar_tensor_tensor(gla["ke"][:, c, :s.tq], psum_w[:, 2 + c, :s.tq], vec[:, VEC["gla", s.layer]][:, c:c + 1],
                                               gla["gr_s"][:, c, :s.tq], ALU.mult, ALU.mult).then_inc(sems["gla_out"], 1)
                    for c in range(2):
                        dve.wait_ge(sems["gla_high"], value("gla_high", s, c + 1))
                        v.tensor_tensor(osplit[:, 1, 2 * s.h + c, :s.tq], gla["ke"][:, c, :s.tq],
                                        osplit[:, 0, 2 * s.h + c, :s.tq].bitcast(F32), ALU.subtract).then_inc(sems["gla_low"], 1)

            def low_of_norm(s, c):
                dve.wait_ge(sems["norm_high"], value("norm_high", s, c + 1))
                v.tensor_tensor(hsplit[:, 1, c, :s.tn], nrm["xn"][:, c, :s.tn], hsplit[:, 0, c, :s.tn].bitcast(F32), ALU.subtract)\
                    .then_inc(sems["norm_low"], 1)

            def attention(s):
                nq = s.tq // P
                n = len(s.heads) * nq
                probs = swa_probs if s.swa else mla_probs
                oc = swa["swa_o"] if s.swa else mla_o
                masked = [0]
                dve.wait_ge(*finished("pe", s.i - 1))
                dve.wait_ge(*finished("act", s.i - 1))
                dve.wait_ge(*finished("dve", s.i - 1))
                dve.wait_ge(*finished("pool", s.i - 1))

                def maximum(i):
                    qt = i % nq
                    keys = slice(0, T) if qt < 2 else slice(NLAT, T)
                    dve.wait_ge(sems["att_scores"], value("att_scores", s, i + 1))
                    if s.swa and qt < 2:
                        far = psum_g[:, i % 4, P * (1 - qt):P * (2 - qt)]
                        v.tensor_tensor(far, far, C["band"][:, qt * P:(qt + 1) * P], ALU.add).then_inc(sems["att_masked"], 1)
                        masked[0] += 1
                        dve.wait_ge(sems["att_masked"], value("att_masked", s, masked[0]))
                    v.tensor_reduce(stats[:, 0, i:i + 1], psum_g[:, i % 4, keys], AX.X, ALU.max, negate=True).then_inc(sems["att_max"], 1)
                    if s.swa:
                        hd = s.heads[i // nq]
                        dve.wait_ge(sems["att_max"], value("att_max", s, i + 1))
                        v.tensor_scalar(stats[:, 1, i:i + 1], stats[:, 0, i:i + 1], nsink[:, s.layer, hd:hd + 1], None, ALU.min)\
                            .then_inc(sems["att_sunk"], 1)

                def normalise(i):
                    keys = slice(0, T) if i % nq < 2 else slice(NLAT, T)
                    total = stats[:, 2, i:i + 1]
                    dve.wait_ge(sems["att_exp"], value("att_exp", s, i + 1))
                    if s.swa:
                        dve.wait_ge(sems["att_exp_sink"], value("att_exp_sink", s, i + 1))
                        v.tensor_tensor(stats[:, 4, i:i + 1], stats[:, 2, i:i + 1], stats[:, 3, i:i + 1], ALU.add).then_inc(sems["att_total"], 1)
                        dve.wait_ge(sems["att_total"], value("att_total", s, i + 1))
                        total = stats[:, 4, i:i + 1]
                    v.reciprocal(stats[:, 5, i:i + 1], total).then_inc(sems["att_inverse"], 1)
                    dve.wait_ge(sems["att_inverse"], value("att_inverse", s, i + 1))
                    v.tensor_scalar(probs[i % len(probs)][:, keys], probs[i % len(probs)][:, keys], stats[:, 5, i:i + 1], None, ALU.mult).then_inc(sems["att_p"], 1)

                def low(hh):
                    dve.wait_ge(sems["att_high"], value("att_high", s, hh + 1))
                    v.tensor_tensor(osplit[:, 1, s.heads[hh], :s.tq], oc[:, :s.tq], osplit[:, 0, s.heads[hh], :s.tq].bitcast(F32),
                                    ALU.subtract).then_inc(sems["att_low"], 1)

                for i in range(n):
                    maximum(i)
                    if i:
                        normalise(i - 1)
                    if i >= nq + 2 and (i - 2) % nq == 0:
                        low((i - 2) // nq - 1)
                normalise(n - 1)
                for hh in range((n - 3) // nq, len(s.heads)):
                    low(hh)

            dve.wait_ge(sems["consts_in"], 48)
            v.memset(tiny[:], EPS).then_inc(sems["init_dve"], 1)
            for l in range(DEPTH):
                v.tensor_scalar(nsink[:, l, :], vec[:, VEC["sink", l]], -1.0, None, ALU.mult).then_inc(sems["init_dve"], 1)
            dve.wait_ge(sems["init_dve"], 3)
            next_split = -1
            for s in steps:
                if s.block is not None and blocks[s.block].split:
                    next_split = max(next_split, split_of[id(blocks[s.block])])
                split_weights(s, next_split if s.i > opening else -2)
                if s.kind in GEMMS:
                    evacuate(s)
                elif s.kind == "ada":
                    if not s.opens:
                        reduce_columns(s, s.u - 1)
                elif s.kind == "mod":
                    l = s.layer
                    reduce_columns(s, s.u)
                    dve.wait_ge(sems["mod_reduced"], value("mod_reduced", s, 1))
                    new = (slice(0, 2 * KC), slice(2 * KC, 6 * KC), slice(0, 6 * KC))[s.q]
                    bias = vec[:, VEC["ada_b", l]][:, new]
                    v.tensor_tensor(mod[:, l, new], mod[:, l, new], bias.unsqueeze(2).broadcast_to([P, new.stop - new.start, 2]), ALU.add)\
                        .then_inc(sems["mod_final"], 1)
                    dve.wait_ge(sems["mod_final"], value("mod_final", s, 1))
                    for m, name in ((0, "mix"), (1, "mlp")):
                        if s.q in (m, 2):
                            first = (3 * m + 1) * KC
                            v.scalar_tensor_tensor(gain[:, l, m], mod[:, l, first:first + KC, :], 1.0,
                                                   vec[:, VEC[name, l]].unsqueeze(2).broadcast_to([P, KC, 2]), ALU.add, ALU.mult)\
                                .then_inc(sems["mod_final"], 1)
                elif s.kind == "norm":
                    dve.wait_ge(*finished("pe", s.i - 1))
                    dve.wait_ge(*finished("act", s.i - 1))
                    dve.wait_ge(*finished("dve", s.i - 1))
                    dve.wait_ge(*finished("pool", s.i - 1))
                    dve.wait_ge(sems["norm_squares"], value("norm_squares", s, 1))
                    v.tensor_reduce(nrm["rinv"][:, :s.tn], nrm["xn"][:, :, :s.tn].rearrange("p c t -> p t c"), AX.X, ALU.add).then_inc(sems["norm_reduced"], 1)
                    dve.wait_ge(sems["norm_root"], value("norm_root", s, 1))
                    v.reciprocal(nrm["rinv"][:, :s.tn], nrm["root"][:, :s.tn]).then_inc(sems["norm_inverse"], 1)
                    dve.wait_ge(sems["norm_inverse"], value("norm_inverse", s, 1))
                    final = s.which == "final"
                    for c in range(KC):
                        gain_c = vec[:, VEC["final", 0]][:, c:c + 1] if final else 1.0
                        v.scalar_tensor_tensor(nrm["xn"][:, c, :s.tn], x[:, c, :s.tn], gain_c, nrm["rinv"][:, :s.tn], ALU.mult, ALU.mult)\
                            .then_inc(sems["norm_scaled"], 1)
                        if not final and c:
                            low_of_norm(s, c - 1)
                    if not final:
                        low_of_norm(s, KC - 1)
                elif s.kind == "cnorm":
                    dve.wait_ge(*finished("pe", s.i - 1))
                    dve.wait_ge(*finished("act", s.i - 1))
                    dve.wait_ge(*finished("dve", s.i - 1))
                    dve.wait_ge(*finished("pool", s.i - 1))
                    groups = ((0, 3, s.tq), (3, 5, T))
                    for i, (a, b, tn) in enumerate(groups):
                        dve.wait_ge(sems["lat_squares"], value("lat_squares", s, i + 1))
                        v.tensor_reduce(lat_sum[:, i, :tn], lat["cx_sq"][:, a:b, :tn].rearrange("p c t -> p t c"), AX.X, ALU.add).then_inc(sems["lat_reduced"], 1)
                    for i, (a, b, tn) in enumerate(groups):
                        dve.wait_ge(sems["lat_root"], value("lat_root", s, i + 1))
                        v.reciprocal(lat_sum[:, i, :tn], lat["cx_sq"][:, i, :tn]).then_inc(sems["lat_inverse"], 1)
                    dve.wait_ge(sems["lat_inverse"], value("lat_inverse", s, 2))
                    v.tensor_tensor(lat["cx_sq"][:, 2, 0:NLAT], kr[:, 0:NLAT], C["mla_cos"], ALU.mult).then_inc(sems["lat_rope"], 1)
                    v.stream_shuffle(lat["cx_sq"][:, 3, 0:NLAT], kr[:, 0:NLAT], [(r + 16) % 32 for r in range(32)]).then_inc(sems["lat_rope"], 1)
                    dve.wait_ge(sems["lat_rope"], value("lat_rope", s, 2))
                    v.tensor_tensor(lat["cx_sq"][:, 3, 0:NLAT], lat["cx_sq"][:, 3, 0:NLAT], C["mla_sin"], ALU.mult).then_inc(sems["lat_rope"], 1)
                    for c in range(5):
                        tn, i = (s.tq, 0) if c < 3 else (T, 1)
                        wc = vec[:, VEC["mq", s.layer]][:, c:c + 1] if c < 3 else vec[:, VEC["mkv", s.layer]][:, c - 3:c - 2]
                        v.scalar_tensor_tensor(lat["cx"][:, c, :tn], lat["cx"][:, c, :tn], wc, lat_sum[:, i, :tn], ALU.mult, ALU.mult).then_inc(sems["lat_scaled"], 1)
                    for c in range(5):
                        tn = s.tq if c < 3 else T
                        dve.wait_ge(sems["lat_high"], value("lat_high", s, c + 1))
                        v.tensor_tensor(mla["cn_r"][:, 1, c, :tn], lat["cx"][:, c, :tn], mla["cn_r"][:, 0, c, :tn].bitcast(F32), ALU.subtract).then_inc(sems["lat_low"], 1)
                elif s.kind == "merge":
                    dve.wait_ge(*finished("pe", s.i - 1))
                    dve.wait_ge(*finished("act", s.i - 1))
                    dve.wait_ge(*finished("dve", s.i - 1))
                    dve.wait_ge(*finished("pool", s.i - 1))
                    for c in range(KC):
                        dve.wait_ge(sems["merge_high"], value("merge_high", s, c + 1))
                        v.tensor_tensor(hsplit[:, 1, c, :s.tq], mg[:, c, :s.tq], hsplit[:, 0, c, :s.tq].bitcast(F32), ALU.subtract).then_inc(sems["merge_low"], 1)
                elif s.kind[:3] == "gla":
                    gla_part(s)
                elif s.kind == "attn":
                    attention(s)

        @block.gpsimd
        def _(pool):
            gp = nc.gpsimd
            for rows in (slice(32, 64), slice(64, 128)):
                gp.memset(zt[rows, :], 0.0).then_inc(sems["zt_ready"], 1)
            pool.wait_ge(sems["zt_ready"], 2)
            gp.memset(zt[32:33, :], 1.0).then_inc(sems["zt_ready"], 1)
            pool.wait_ge(sems["zt_ready"], 3)
            for s in steps:
                if not counts(s).get("pool"):
                    continue
                k = s.kind
                pool.wait_ge(*finished("pool", s.i - 1))
                if k in GEMMS:
                    pool.wait_ge(*finished("pe", s.after))
                    pool.wait_ge(*finished("act", s.after))
                    pool.wait_ge(*finished("dve", s.after))
                if k in ("sq", "sk"):
                    pool.wait_ge(sems["dve_rope"], value("dve_rope", s, 5))
                    dst = swa["sq_s"][:, 2 * s.j:2 * s.j + 2, 0:NLAT] if k == "sq" else swa["sk_s"][:, :, 0:NLAT]
                    gp.tensor_tensor(dst, swa["rp"][:, 0], swa["rp"][:, 1], ALU.add).then_inc(sems["pool_evac"], 1)
                elif k == "uqp":
                    pool.wait_ge(sems["dve_rope"], value("dve_rope", s, 3))
                    gp.tensor_tensor(mla["qp"][:, 0:NLAT], mla["mla_p"][:, 0, 0:NLAT], mla["mla_p"][:, 1, 0:NLAT], ALU.add).then_inc(sems["pool_evac"], 1)
                elif k == "branch":
                    pool.wait_ge(sems["dve_evac"], value("dve_evac", s, 1))
                    dst = mg[:, 2 * s.j:2 * s.j + 2, :s.t]
                    gp.tensor_tensor(dst, dst, br["bt"][:, s.j % 2, :, :s.t], ALU.add).then_inc(sems["pool_evac"], 1)
                elif k == "up":
                    pool.wait_ge(sems["act_evac"], value("act_evac", s, 1))
                    r = ups["rt"][:, s.j % 2, :, :s.t]
                    gp.tensor_tensor(r, r, r, ALU.mult).then_inc(sems["pool_evac"], 1)
                elif k in ("gla1", "gla2"):
                    before_it = s.i - 1 if s.h == 0 and k == "gla1" else s.needs
                    pool.wait_ge(*finished("pe", before_it))
                    pool.wait_ge(*finished("act", before_it))
                    pool.wait_ge(*finished("dve", before_it))
                    h2 = s.h % 2
                    if k == "gla1":
                        gp.memset(gla["at"][:], 0.0).then_inc(sems["gla_zeroed"], 1)
                        gp.memset(gla["ktp"][:], 0.0).then_inc(sems["gla_zeroed"], 1)
                    else:
                        for d in range(2):
                            pool.wait_ge(sems["gla_exps"], value("gla_exps", s, 2 * (d + 1)))
                            gp.tensor_tensor(gla["qd"][:, d, :s.tq], gla["gq_s"][:, h2, :s.tq], gla["ep"][:, d, :s.tq], ALU.mult)\
                                .then_inc(sems["gla_qdec"], 1)
                        for d in range(2):
                            pool.wait_ge(sems["gla_exp_end"], value("gla_exp_end", s, d + 1))
                            gp.tensor_tensor(gla["ke"][:, d, :], gla["gk_s"][:, h2, :], gla["ke"][:, d, :], ALU.mult)\
                                .then_inc(sems["gla_kend"], 1)
                elif k == "cnorm":
                    pool.wait_ge(*finished("pe", s.i - 1))
                    pool.wait_ge(*finished("act", s.i - 1))
                    pool.wait_ge(*finished("dve", s.i - 1))
                    pool.wait_ge(*finished("pool", s.i - 1))
                    for a in range(2):
                        rows = slice(64 * (1 - a), 64 * (1 - a) + 64)
                        gp.memset(kpe[rows, a, :], 0.0).then_inc(sems["lat_zeroed"], 1)
                    pool.wait_ge(sems["lat_rope"], value("lat_rope", s, 3))
                    for a in range(2):
                        rows = slice(64 * a, 64 * a + 64)
                        gp.tensor_tensor(kpe[rows, a, 0:NLAT], lat["cx_sq"][rows, 2, 0:NLAT], lat["cx_sq"][rows, 3, 0:NLAT], ALU.add).then_inc(sems["lat_k_roped"], 1)


def constants():
    c = np.zeros((P, NCONST), np.float32)
    c[:, CONST["ident"]] = np.eye(P)
    c[:, CONST["ones"]] = 1.0
    t = np.arange(P)
    same = t[:, None] // GLA_CHUNK == t[None, :] // GLA_CHUNK
    c[:, CONST["tri"]] = np.concatenate([same & (t[:, None] <= t), same & (t[:, None] >= t)], 1) / 16.0
    c[:, CONST["band"]] = np.where(np.concatenate([t <= t[:, None], t >= t[:, None]], 1), 0.0, NEG)
    row, col = np.arange(NLAT) // 64, np.arange(NLAT) % 64

    def tables(half):
        inv = np.float32(10000.0) ** (-np.arange(0, 2 * half, 2, dtype=np.float32) / np.float32(2 * half))
        angle = [(inv[:, None] * pos.astype(np.float32)).astype(np.float32) for pos in (row, col)]
        cos = np.concatenate([np.cos(a) for a in angle for _ in range(2)])
        sin = np.concatenate([s * np.sin(a) for a in angle for s in (-1, 1)])
        return cos.astype(np.float32), sin.astype(np.float32)

    cos, sin = tables(32)
    c[:, CONST["swa_cos"]] = cos
    c[:, CONST["swa_sin"]] = sin.reshape(4, 32, NLAT)[[1, 0, 3, 2]].reshape(P, NLAT)
    cos, sin = tables(16)
    c[:, CONST["mla_cos"]] = np.concatenate([cos, cos])
    c[:, CONST["mla_sin"]] = np.concatenate([sin, sin])
    return c


def weight_block(b, w):
    l, j = b.layer, b.j
    win = w["w_in"][l]

    def cols(name, n, width=256):
        return win[:, OFF[name] + n * width:OFF[name] + (n + 1) * width]

    if b.name == "ada":
        m = w["ada_w"][l][:, j * 256:(j + 1) * 256]
    elif b.name == "zk":
        kr = cols("kr", 0, 64)
        m = np.concatenate([cols("gzf", 0, 32), np.zeros((D, 96), win.dtype), kr, kr], 1)
    elif b.name == "cq":
        m = (cols("cq", 0), cols("ckv", 0), cols("cq", 2, 128))[j]
    elif b.name in OFF:
        m = cols(b.name, j)
    elif b.name == "gate":
        m = cols("gates", 4 * b.part + j)
    elif b.name == "branch":
        m = w["w_branch"][l, b.part][:, j * 256:(j + 1) * 256]
    elif b.name == "out":
        m = w["w_out"][l][:, j * 256:(j + 1) * 256]
    elif b.name == "up":
        m = w["mlp_w1"][l][:, b.part * QUARTER + j * 256:b.part * QUARTER + (j + 1) * 256]
    elif b.name == "down":
        m = w["mlp_w2"][l][b.part * QUARTER:(b.part + 1) * QUARTER, j * 256:(j + 1) * 256]
    elif b.name == "uv":
        m = w["mla_w_ukv"][l].reshape(MLA_KV, 8, 2, HEAD)[:, 2 * j:2 * j + 2].transpose(0, 2, 1, 3).reshape(MLA_KV, 512)
    else:
        h = w["mla_w_uq"][l].reshape(MLA_Q, 8, 192)[:, 2 * j:2 * j + 2]
        m = np.concatenate([h[:, 0, :HEAD], h[:, 1, :HEAD], h[:, 0, HEAD:], h[:, 1, HEAD:]], 1)
    return m.reshape(-1, P, m.shape[1]).transpose(1, 0, 2)


def chunked(v):
    return v.reshape(-1, P).T


def kernel(**inputs):
    import concourse.bacc as bacc
    from concourse.bass_utils import run_bass_kernel_spmd

    w = {k: np.asarray(v) for k, v in inputs.items()}
    tokens = np.concatenate([w["x"][0], w["ctx"][0]], 0)
    cvec = np.zeros((P, KC, 32), np.float32)
    cvec[:, :, 0] = chunked(w["c"][0])
    cvec[:, :, 1] = chunked(w["c_ctx"])
    vectors = np.zeros((P, NVEC), np.float32)
    decay = np.zeros((DEPTH, P, 2, 512), np.float32)
    for l in range(DEPTH):
        for name, key in (("mix", "norm_mix_w"), ("mlp", "norm_mlp_w"), ("ada_b", "ada_b"), ("gla", "gla_norm_w"),
                          ("mq", "mla_q_norm_w"), ("mkv", "mla_kv_norm_w")):
            vectors[:, VEC[name, l]] = chunked(w[key][l])
        vectors[:, VEC["sink", l]] = w["swa_sink"][l][None, :]
        for d in range(2):
            decay[l, d * GLA_RANK:(d + 1) * GLA_RANK, d] = w["gla_a_w"][l, d]
            decay[l, 2 * GLA_RANK, d] = w["gla_a_b"][l, d]
    vectors[:, VEC["final", 0]] = chunked(w["final_norm_w"])
    _, blocks = plan()
    weights = np.empty(P * sum(b.size for b in blocks), np.float32)
    at = 0
    for b in blocks:
        m = weight_block(b, w)
        assert m.shape[1] * m.shape[2] == b.size, (b, m.shape)
        weights[at:at + m.size].reshape(m.shape)[...] = m
        at += m.size
    arrays = dict(xt=np.ascontiguousarray(tokens.T.reshape(KC, P, T).transpose(1, 0, 2)), cvec=cvec, consts=constants(),
                  vectors=vectors, decay_w=decay, weights=weights)

    nc = bacc.Bacc("TRN2", target_bir_lowering=False, num_devices=1)
    args = {n: nc.dram_tensor(n, a.shape, F32, kind="ExternalInput").ap() for n, a in arrays.items()}
    out = nc.dram_tensor("out", (P, KC, NLAT), F32, kind="ExternalOutput").ap()
    build(nc, out=out, **args)
    r = run_bass_kernel_spmd(nc, [arrays], core_ids=[0])
    got = r.results[0]["out"]
    return got.transpose(1, 0, 2).reshape(D, NLAT).T.reshape(1, NLAT, D)
```

```python
from contextlib import ExitStack

import numpy as np

import concourse.bass as bass
from concourse import mybir

F32 = mybir.dt.float32
F32R = mybir.dt.float32r
U32 = mybir.dt.uint32
ALU = mybir.AluOpType
ACT = mybir.ActivationFunctionType
AX = mybir.AxisListType



class Step:

    def __init__(self, i, kind, layer, j=0, branch=0, q=0, h=0, heads=(), which=None, tn=0, tq=0, swa=False):
        self.i, self.kind, self.layer = i, kind, layer
        self.j, self.branch, self.q = j, branch, q
        self.h, self.heads, self.swa = h, heads, swa
        self.which, self.tn, self.tq = which, tn, tq
        self.block = None
        self.tiles, self.t, self.kc = 0, T, KC
        self.needs = self.after = -1
        self.pair, self.banks_of = 0, -1
        self.bank0 = 0
        self.scores = None
        self.u, self.opens = 0, False
        self.frees = -1
        self.a0 = 0


class Block:

    def __init__(self, name, layer, j, part, size, split):
        self.name, self.layer, self.j, self.part, self.size, self.split = name, layer, j, part, size, split
        self.first = self.last = None


P = 128
D = 1024
KC = D // P
NLAT = 256
T = 512
DEPTH = 2
EPS = 1e-6
GLA_HEADS, GLA_DK, GLA_DV, GLA_CHUNK, GLA_RANK = 4, 128, 256, 64, 16
NCH = T // GLA_CHUNK
HEAD = 128
SWA_SCALE = HEAD ** -0.5
MLA_SCALE = (128 + 64) ** -0.5
MLA_Q, MLA_KV = 384, 256
FF = 4 * D
QUARTER = FF // 4
NEG = -1e30
SLOT = KC * 2 * P
NRAW = 2
NSPLIT = 2
AHEAD = 3
NP_SWA = 3

OFF = dict(zip(("gq", "gk", "gv", "gr", "gzf", "gzb", "sq", "sk", "sv", "cq", "ckv", "kr", "gates"),
               np.cumsum([0, 512, 512, 1024, 1024, 16, 16, 1024, 256, 256, 384, 256, 64]).tolist()))

CONST = {}
_at = 0
for _name, _n in (("ident", P), ("ones", P), ("tri", 2 * P), ("band", 2 * P), ("swa_cos", NLAT),
                  ("swa_sin", NLAT), ("mla_cos", NLAT), ("mla_sin", NLAT)):
    CONST[_name] = slice(_at, _at + _n)
    _at += _n
NCONST = _at

VEC = {}
_at = 0
for _l in range(DEPTH):
    for _name, _n in (("mix", KC), ("mlp", KC), ("ada_b", 6 * KC), ("gla", 2), ("mq", 3), ("mkv", 2), ("sink", 8)):
        VEC[_name, _l] = slice(_at, _at + _n)
        _at += _n
VEC["final", 0] = slice(_at, _at + KC)
NVEC = _at + KC

GEMMS = ("zk", "gq", "gk", "gv", "gr", "sq", "sk", "sv", "cq", "ukn", "uv", "uqn", "uqp",
         "gate", "branch", "out", "up", "down")


def plan():
    steps, blocks = [], []
    last_stage = [-1]

    def add(kind, **kw):
        s = Step(len(steps), kind, **kw)
        s.after = max(last_stage[0], s.i - 2)
        steps.append(s)
        return s

    def stage(kind, **kw):
        s = add(kind, **kw)
        last_stage[0] = s.i
        return s

    def block(name, layer, j, part, size, split=True):
        blocks.append(Block(name, layer, j, part, size, split))
        return len(blocks) - 1

    def fill(calls, n):
        for _ in range(n):
            next(calls, lambda: None)()

    def gemm(kind, l, j, t=T, size=SLOT, tiles=2, old=None, kc=KC, needs=-1, a0=0, **kw):
        s = add(kind, layer=l, j=j, **kw)
        s.block = block(kind, l, j, kw.get("branch", kw.get("q", 0)), size) if old is None else old
        s.t, s.tiles, s.kc, s.needs, s.a0 = t, tiles, kc, needs, a0
        b = blocks[s.block]
        b.first = s.i if b.first is None else b.first
        b.last = s.i
        return s

    ada = [0]

    def squares(l, j, tn, after):
        add("squares", layer=l, j=j, tn=tn).after = after

    def modulation(l, j, first=False):
        s = add("ada", layer=l, j=j)
        s.u, s.opens, s.after = ada[0], first, last_stage[0]
        ada[0] += 1
        s.block = block("ada", l, j, 0, SLOT, split=False)
        blocks[s.block].first = blocks[s.block].last = s.i

    def modulations(l, blocks_of_l):
        for j in blocks_of_l:
            yield lambda j=j: modulation(l, j, j == blocks_of_l[0])

    for j in range(8):
        modulation(0, j, j == 0)
        if j % 2:
            squares(0, j // 2, T, -1)
    stage("mod", layer=0, q=0).u = 7
    extra = modulations(0, range(8, 24))
    for l in range(DEPTH):
        tq = T if l < DEPTH - 1 else NLAT
        norm = stage("norm", layer=l, which="mix", tn=T)
        gemm("zk", l, 0, needs=norm.i)
        queries = gemm("gq", l, 0, t=tq, tiles=1)
        first = stage("gla1", layer=l, h=0, tq=tq)
        first.needs = queries.i
        last_part = gemm("gk", l, 0, tiles=1, old=queries.block, a0=1)
        for h in range(GLA_HEADS):
            second = stage("gla2", layer=l, h=h, tq=tq)
            second.needs, second.frees = last_part.i, (last_part.i if h == 0 else fourth.i)
            values = gemm("gv", l, h, tiles=1)
            gemm("gv", l, h, tiles=1, old=values.block, a0=1)
            third = stage("gla3", layer=l, h=h, tq=tq)
            third.needs = second.i
            gains = gemm("gr", l, h, t=tq, tiles=1)
            if h + 1 < GLA_HEADS:
                first = stage("gla1", layer=l, h=h + 1, tq=tq)
                first.needs = third.i
            gemm("gr", l, h, t=tq, tiles=1, old=gains.block, a0=1)
            if h + 1 < GLA_HEADS:
                queries = gemm("gq", l, h + 1, t=tq, tiles=1)
            fourth = stage("gla4", layer=l, h=h, tq=tq)
            fourth.needs, fourth.frees = max(first.i, third.i), third.i
            if h + 1 < GLA_HEADS:
                gemm("gk", l, h + 1, tiles=1, old=queries.block, a0=1)
            else:
                gemm("gate", l, 0, t=tq, branch=0)
            mixed = last_part = stage("gla5", layer=l, h=h, tq=tq)
            last_part.needs = fourth.i

        def gate(b, j):
            if b or j:
                gemm("gate", l, j, t=tq, branch=b)
                fill(extra, 1)

        def branch(b, j, mixed):
            s = gemm("branch", l, j, t=tq, branch=b, needs=mixed.i if j == 0 else -1)
            fill(extra, 1)
            return s

        def branches(b, mixed, n=4):
            for j in range(n):
                gate(b, j)
                branch(b, j, mixed)

        def merge(j, last_gate, product):
            s = add("merge", layer=l, j=j, tq=tq)
            s.after, s.needs = last_gate, product.i
            return s

        branches(0, mixed)
        keys = gemm("sk", l, 0)
        keys.after = keys.i - 1
        fill(extra, 1)
        rope = keys
        for p in range(4):
            query = gemm("sq", l, p, t=tq)
            query.after = max(query.after, rope.i)
            rope = query
            fill(extra, 1)
        gemm("sv", l, 0)
        mixed = stage("attn", layer=l, heads=range(8), tq=tq, swa=True)
        branches(1, mixed, 3)
        gate(1, 3)
        if l == 0:
            stage("mod", layer=0, q=1).u = 23
        gemm("cq", l, 2, t=tq, size=SLOT // 2, tiles=1)
        gemm("cq", l, 0, t=tq)
        gemm("cq", l, 1)
        squared = add("csum", layer=l, tq=tq)
        branch(1, 3, mixed)
        latent = stage("cnorm", layer=l, tq=tq)
        latent.needs = squared.i
        for p in range(4):
            s = gemm("uqn", l, p, size=3 * 384, kc=3, t=tq, needs=latent.i if p == 0 else -1)
            if p == 0:
                stage("krope", layer=l)
            gemm("uqp", l, p, kc=3, t=tq, tiles=1, old=s.block)
            s = gemm("ukn", l, p, size=2 * 512, kc=2, needs=latent.i if p == 0 else -1)
            gemm("uv", l, p, kc=2, old=s.block)
            mixed = stage("attn", layer=l, heads=range(2 * p, 2 * p + 2), tq=tq, swa=False)
        done = []
        for j in range(2):
            gate(2, j)
            done.append(branch(2, j, mixed))
        gate(2, 2)
        gate(2, 3)
        last_gate = steps[-1].i
        merged = [merge(0, last_gate, done[0]), merge(1, last_gate, done[1])]
        done += [branch(2, 2, mixed), branch(2, 3, mixed)]
        merge(2, last_gate, done[2])
        merge(3, last_gate, done[3])
        for j in range(4):
            s = gemm("out", l, j, t=tq, needs=merged[0].i if j == 0 else -1)
            squares(l, j, tq, s.i)
        norm = stage("norm", layer=l, which="mlp", tn=tq)
        extra = modulations(l + 1, range(24) if l + 1 < DEPTH else ())
        up = {}
        down = {}
        for q, kind in ((0, "up"), (1, "up"), (0, "down"), (2, "up"), (1, "down"), (3, "up"), (2, "down"), (3, "down")):
            for j in range(4):
                if kind == "up":
                    s = gemm("up", l, j, t=tq, q=q, needs=norm.i if (q, j) == (0, 0) else -1)
                    if q >= 2:
                        s.after = max(s.after, down[q - 2].i)
                    up[q] = s
                else:
                    down[q] = gemm("down", l, j, t=tq, q=q, needs=up[q].i if j == 0 else -1)
                    if q == 3:
                        squares(l, j, tq, down[q].i)
                fill(extra, 1)
        if l + 1 < DEPTH:
            stage("mod", layer=l + 1, q=2).u = 47
    stage("norm", layer=0, which="final", tn=NLAT)
    products = [s for s in steps if s.kind in GEMMS]
    for n, s in enumerate(products):
        s.pair = n % 2
        s.banks_of = products[n - 2].i if n >= 2 else -1
        s.scores = next((a for a in steps[:s.i] if a.kind == "attn" and a.i > s.banks_of), None)
    for s in steps:
        if s.kind == "attn":
            s.bank0 = 2 * (1 - steps[s.i - 1].pair)
    return steps, blocks


def runs(blocks):
    out = []
    for b in blocks:
        if out and out[-1][0] == b.size:
            out[-1][1] += 1
        else:
            out.append([b.size, 1])
    return out


def counts(s):
    k = s.kind
    nq = s.tq // P
    if k == "ada":
        return dict(pe=[("mod_columns", 1)] * (not s.opens), act=[("mod_copied", 1)],
                    dve=[("mod_reduced", 1)] * (not s.opens))
    if k == "mod":
        return dict(pe=[("mod_columns", 1)], dve=[("mod_reduced", 1), ("mod_final", (2, 2, 3)[s.q])])
    if k == "norm":
        if s.which == "final":
            return dict(pe=[("norm_sum", 1)], act=[("table", 1), ("norm_root", 1)], dve=[("norm_inverse", 1), ("norm_scaled", KC)])
        return dict(pe=[("norm_sum", 1)], act=[("table", 1), ("norm_root", 1), ("norm_shifted", KC), ("norm_high_odd", KC // 2)],
                    dve=[("norm_inverse", 1), ("norm_scaled", KC // 2), ("norm_high", KC // 2), ("norm_low", KC)],
                    pool=[("norm_scaled_odd", KC // 2)])
    if k == "squares":
        return dict(act=[("norm_squares", 2)]) if s.j == 3 else dict(pool=[("norm_partial", 4 if s.j else 3)])
    if k == "gla1":
        return dict(pe=[("gla_z", 2)], act=[("gla_abs", 2), ("gla_exp_z", 1), ("gla_ln", 2)], dve=[("gla_la", 2)],
                    pool=[("gla_zeroed", 2)] if s.h == 0 else [])
    if k == "gla2":
        return dict(pe=[("gla_sums", 2)], act=[("gla_exps", 4), ("gla_exp_end", 2)],
                    dve=[("gla_last", 2), ("gla_to_end", 2), ("gla_kinv", 2)], pool=[("gla_qdec", 2), ("gla_kend", 2)])
    if k == "gla3":
        return dict(pe=[("gla_kend_t", 2), ("gla_a", 2)], act=[("gla_kend_s", 4)], dve=[("gla_masked", 2)])
    if k == "gla4":
        return dict(pe=[("gla_u", NCH - 1), ("gla_o", 1)], act=[("table", 1), ("gla_sumsq", nq), ("gla_root", 1)],
                    dve=[("gla_state", 2 * (NCH - 1)), ("gla_inverse", 1), ("gla_o_s", nq)])
    if k == "gla5":
        return dict(pe=[("gla_o_t", 1)], act=[("gla_high", 2)], dve=[("gla_out", 2), ("gla_low", 2)])
    if k == "attn":
        n = len(s.heads) * nq
        masked = [("att_masked", 2 * len(s.heads)), ("att_sunk", n), ("att_total", n)] if s.swa else []
        return dict(pe=[("att_scores", n), ("att_p_t", n), ("att_pv", n)],
                    act=[("att_exp", n)] + [("att_exp_sink", n)] * s.swa + [("att_p_s", n), ("att_o_s", len(s.heads)), ("att_high", len(s.heads))],
                    dve=masked + [("att_max", n), ("att_inverse", n), ("att_p", n), ("att_low", len(s.heads))])
    if k == "csum":
        return dict(act=[("lat_squares", 2)], dve=[("lat_reduced", 2)])
    if k == "cnorm":
        return dict(pe=[("lat_sum", 1), ("lat_spread", 2)], act=[("table", 1), ("lat_root", 2), ("lat_high", 5)],
                    dve=[("lat_inverse", 2), ("lat_scaled", 5), ("lat_low", 5)])
    if k == "krope":
        return dict(act=[("lat_kr", 2)], dve=[("lat_rope", 3)], pool=[("lat_zeroed", 2), ("lat_k_roped", 2)])
    if k == "merge":
        return dict(act=[("merge_high", 2)], dve=[("merge_low", 2)])
    e = dict(pe=[("product", s.tiles)])
    ctx = s.t > NLAT
    if k == "gv":
        e.update(dict(dve=[("dve_evac", 1)]) if s.a0 else dict(act=[("act_evac", 1)]))
    elif k == "gq":
        e.update(act=[("act_evac", 1)])
    elif k == "gk":
        e.update(dve=[("dve_evac", 1)])
    elif k in ("zk", "sv", "ukn", "uv", "uqn"):
        e.update(act=[("act_evac", 1)], dve=[("dve_evac", 1)])
    elif k == "cq":
        e.update(act=[("act_evac", 1)], **(dict(dve=[("dve_evac", 1)]) if s.tiles > 1 else {}))
    elif k == "gr":
        e.update(act=[("act_evac", 1)])
    elif k in ("sq", "sk"):
        e.update(dve=[("dve_rope", 5)], pool=[("pool_evac", 1)], **(dict(act=[("act_evac", 1)]) if ctx else {}))
    elif k == "uqp":
        e.update(dve=[("dve_rope", 3)], pool=[("pool_evac", 1)], **(dict(act=[("act_evac", 1)]) if ctx else {}))
    elif k == "gate":
        e.update(act=[("act_evac", 2)])
    elif k == "branch":
        e.update(dve=[("dve_evac", 1)], **(dict(pool=[("pool_evac", 1)]) if s.branch else {}))
    elif k == "up":
        e.update(act=[("act_evac", 1), ("up_high", 1)], dve=[("dve_evac", 1), ("up_low", 1)])
    else:
        e.update(dve=[("dve_evac", 2 * (s.t // NLAT))])
    return e


def build(nc, xt, cvec, consts, vectors, decay_w, weights, out):
    steps, blocks = plan()
    ENGINES = ("pe", "act", "dve", "pool")

    before, ends, running = [], {e: [] for e in ENGINES}, {}
    last = {e: None for e in ENGINES}
    for s in steps:
        before.append(dict(running))
        for e, names in counts(s).items():
            for name, n in names:
                running[name] = running.get(name, 0) + n
            if names:
                last[e] = (names[-1][0], running[names[-1][0]])
        for e in ENGINES:
            ends[e].append(last[e])

    def value(name, s, n):
        return before[s.i].get(name, 0) + n

    def finished(engine, i):
        name, count = (ends[engine][i] if i >= 0 else None) or ("consts_in", 32)
        return sems[name], count

    split_of = {}
    for b in blocks:
        if b.split:
            split_of[id(b)] = len(split_of)
    split_blocks = [b for b in blocks if b.split]

    def room_for(n, s):
        m = blocks.index(split_blocks[n]) - NRAW
        if s.kind in ("gq", "gla4") and split_blocks[n].first > s.i:
            return False
        return (n < NSPLIT or split_blocks[n - NSPLIT].last < s.i) and (m < 0 or blocks[m].split or blocks[m].last < s.i)

    with ExitStack() as ctx:
        top = [(nc.sbuf_base + 63) // 64 * 64]

        def fixed(name, shape, dt=F32):
            n = 4 * int(np.prod(shape[1:]))
            t = nc.alloc_sbuf_tensor_at(name, shape, dt, offset=top[0])
            top[0] += (n + 63) // 64 * 64
            return t

        x = fixed("x", [P, KC, T])
        hsplit = fixed("hsplit", [P, 2, KC, T], F32R)
        o_base = top[0]
        osplit = fixed("osplit", [P, 2, KC, T], F32R)
        wsplit = fixed("wsplit", [P, NSPLIT, 2, SLOT], F32R)
        raw = fixed("raw", [P, NRAW, SLOT])
        cst = fixed("cst", [P, NCONST])
        vec = fixed("vec", [P, NVEC])
        dw_base = top[0]
        dw = fixed("dw", [P, 2, 512])
        zt = fixed("zt", [P, T])
        kr = fixed("kr", [P, T])
        cs = fixed("cs", [P, KC, 32])
        part_base = top[0]
        part = fixed("part", [P, 2, 256])
        mod = fixed("mod", [P, DEPTH, 6 * KC, 2])
        gain = fixed("gain", [P, DEPTH, 2, KC, 2])
        nsink = fixed("nsink", [P, DEPTH, 8])
        tiny = fixed("tiny", [P, 1])
        spare = fixed("spare", [P, 1])
        stats = fixed("stats", [P, 6, 32])
        mg_base = top[0]
        mg = fixed("mg", [P, KC, T])
        scratch = top[0]
        end = nc.sbuf_usable_end

        def region(base, **shapes):
            got, at = {}, base
            for name, shape in shapes.items():
                dt = F32R if name.endswith("_r") else F32
                got[name] = nc.alloc_sbuf_tensor_at(name, [P, *shape], dt, offset=at)
                at += (4 * int(np.prod(shape)) + 63) // 64 * 64
            assert at <= end, (sorted(shapes), at, end)
            return got

        nrm = region(mg_base, xn=(KC, T), root=(T,), rinv=(T,))
        gla = region(mg_base, gq_s=(2, T), gk_s=(2, T), gv_s=(4, 256), gr_s=(2, T), la=(2, T), ep=(2, T),
                     en=(2, T), ke=(2, T), qd=(2, T), ktp=(2, 4, 2, P), at=(2, T), st=(2, 2, 256), last=(2, NCH))
        br = region(scratch, sg=(2, 2, T), bt=(2, 2, T))
        swa = region(scratch, sk_s=(2, T), sv_s=(4, 256), sq_s=(8, T), rp=(2, 2, NLAT), swa_p=(NP_SWA, T), swa_pt=(2, T), swa_o=(T,))
        mla = region(scratch, cn_r=(2, 5, T), kn=(2, T), vm=(4, 256), qn=(2, T), qp=(T,), mla_p=(2, T), mla_pt=(T,), mla_pt2=(T,))
        lat = region(scratch + 4 * 2 * 5 * T, cx=(5, T), cx_sq=(5, T))
        lat_sum = nc.alloc_sbuf_tensor_at("lat_sum", [P, 2, T], F32, offset=scratch + 16 * 1024)
        kpe = nc.alloc_sbuf_tensor_at("kpe", [P, 2, T], F32, offset=dw_base)
        mla_o = nc.alloc_sbuf_tensor_at("mla_o", [P, T], F32, offset=part_base)
        hid = [nc.alloc_sbuf_tensor_at("hid0", [P, 2, KC, T], F32R, offset=o_base),
               nc.alloc_sbuf_tensor_at("hid1", [P, 2, KC, T], F32R, offset=mg_base)]
        sums = region(mg_base + 40 * 1024, total=(T,), sq=(3, T))
        ups = region(mg_base + 4 * 2 * KC * T, rt=(2, 2, T), rt_sq=(2, 2, T))

        swa_probs = [swa["swa_p"][:, n, :] for n in range(NP_SWA)]
        mla_probs = [mla["mla_p"][:, 0, :], mla["mla_p"][:, 1, :], kr[:, :]]
        mla_turned = [mla["mla_pt"][:, :], mla["mla_pt2"][:, :]]

        o_s = gla["qd"][:, :, :].rearrange("p a (b n) -> p (a b) n", n=256)

        psum_g = nc.alloc_psum_tensor("psum_g", [P, 4, T], F32)
        psum_w = nc.alloc_psum_tensor("psum_w", [P, 4, T], F32)

        sems = {}
        for name in sorted(running) + ["w_high", "consts_in", "cvec_in", "x_in", "dw_in", "zt_ready", "init_act", "init_dve", "out_done"]:
            sems[name] = ctx.enter_context(nc.semaphore(name))
        raw_in = [ctx.enter_context(nc.semaphore(f"raw_in{n}")) for n in range(NRAW)]
        raw_used = [ctx.enter_context(nc.semaphore(f"raw_used{n}")) for n in range(NRAW)]

        C = {n: cst[:, s] for n, s in CONST.items()}

        def chunk_cols(c):
            return slice(c * GLA_CHUNK, (c + 1) * GLA_CHUNK)

        half = T // GLA_CHUNK // 2
        ORDER = ([*range(half, NCH), *range(half)], [*reversed(range(half, NCH)), *reversed(range(half))])

        def last_col(d, c):
            return c * GLA_CHUNK + (GLA_CHUNK - 1 if d == 0 else 0)

        opening = next(s.i for s in steps if s.kind == "mod")

        block = ctx.enter_context(nc.Block())

        @block.sync
        def _(sp):
            sp.dma_start(cs[:], cvec).then_inc(sems["cvec_in"], 16)
            for n in range(NRAW):
                sp.dma_start(raw[:, n, :], weights[n * P * SLOT:(n + 1) * P * SLOT].rearrange("(p n) -> p n", n=SLOT)).then_inc(raw_in[n], 16)
            sp.dma_start(cst[:], consts).then_inc(sems["consts_in"], 16)
            sp.dma_start(vec[:], vectors).then_inc(sems["consts_in"], 16)

            n, at = 0, 0
            for size, count in runs(blocks):
                stream = weights[at:at + count * P * size].rearrange("(u p n) -> u p n", p=P, n=size)
                at += count * P * size
                k = NRAW if n == 0 else 0
                n += k
                while k < count and n % NRAW:
                    sp.wait_ge(raw_used[n % NRAW], n // NRAW)
                    sp.dma_start(raw[:, n % NRAW, :size], stream[k]).then_inc(raw_in[n % NRAW], 16)
                    k, n = k + 1, n + 1
                pairs = (count - k) // NRAW
                if pairs > 1:
                    with sp.Fori(0, pairs) as i:
                        for r in range(NRAW):
                            sp.wait_ge(raw_used[r], i + n // NRAW)
                            sp.dma_start(raw[:, r, :size], stream[bass.ds(i * NRAW + (k + r), 1)]
                                         .rearrange("u p n -> p (u n)")).then_inc(raw_in[r], 16)
                    k, n = k + pairs * NRAW, n + pairs * NRAW
                while k < count:
                    sp.wait_ge(raw_used[n % NRAW], n // NRAW)
                    sp.dma_start(raw[:, n % NRAW, :size], stream[k]).then_inc(raw_in[n % NRAW], 16)
                    k, n = k + 1, n + 1
            for c in range(KC):
                sp.wait_ge(sems["norm_scaled"], value("norm_scaled", steps[-1], c + 1))
                sp.dma_start(out[:, c, :], nrm["xn"][:, c, 0:NLAT]).then_inc(sems["out_done"], 16)
            sp.wait_ge(sems["out_done"], 16 * KC)

        def arrived(n):
            return raw_in[n % NRAW], 16 * (n // NRAW + 1)

        def used(n):
            return raw_used[n % NRAW], n // NRAW + 1

        @block.tensor
        def _(pe):
            mm, tr = nc.tensor.matmul, nc.tensor.transpose
            g = [psum_g[:, b, :] for b in range(4)]
            w = [psum_w[:, b, :] for b in range(4)]

            def three(dst, a, b, first, final):
                mm(dst, a[0], b[0], start=first, stop=False, skip_group_check=True)
                mm(dst, a[0], b[1], start=False, stop=False, skip_group_check=True)
                return mm(dst, a[1], b[0], start=False, stop=final, skip_group_check=True)

            def product(s):
                b = blocks[s.block]
                n = split_of[id(b)]
                if b.first == s.i:
                    pe.wait_ge(*used(s.block))
                pe.wait_ge(*finished("act", s.banks_of))
                pe.wait_ge(*finished("dve", s.banks_of))
                if s.scores:
                    pe.wait_ge(sems["att_exp"], value("att_exp", s.scores, len(s.scores.heads) * s.scores.tq // P))
                if s.kind in ("down",):
                    act = hid[s.q % 2]
                elif s.kind == "branch":
                    act = osplit
                elif s.kind in ("ukn", "uv", "uqn", "uqp"):
                    act = mla["cn_r"]
                else:
                    act = hsplit
                made = steps[s.needs] if s.needs >= 0 else None
                in_chunks = {"norm": "norm_low", "merge": "merge_low", "cnorm": "lat_low"}.get(made.kind if made else None)
                if made and s.kind == "branch":
                    if made.kind == "attn":
                        pe.wait_ge(sems["att_low"], value("att_low", made, len(made.heads) - 1))
                    else:
                        pe.wait_ge(*finished("dve", made.i - 1))
                elif made and s.kind == "ukn":
                    pe.wait_ge(sems["lat_low"], value("lat_low", made, 5))
                elif made and not in_chunks:
                    pe.wait_ge(*finished("act", s.needs))
                    pe.wait_ge(*finished("dve", s.needs))
                    pe.wait_ge(*finished("pool", s.needs))
                wide = b.size // s.kc
                wv = wsplit[:, n % NSPLIT, :, :b.size].rearrange("p h (k n) -> p h k n", n=wide)
                k0 = {"ukn": 3, "uv": 3}.get(s.kind, 0)
                col0 = {"uv": 256, "uqp": 256}.get(s.kind, 0)
                if in_chunks and s.kind != "ukn":
                    for k in range(s.kc):
                        pe.wait_ge(sems[in_chunks], value(in_chunks, made, k + 1))
                        for a in range(2):
                            ws = [wv[:, i, k, a * P:(a + 1) * P] for i in (0, 1)]
                            hs = [act[:, i, k, 0:s.t] for i in (0, 1)]
                            ins = three(g[2 * s.pair + a][:, 0:s.t], ws, hs, k == 0, k == s.kc - 1)
                    ins.then_inc(sems["product"], 2)
                    return
                for a in range(s.a0, s.a0 + s.tiles):
                    bank = g[2 * s.pair + a - s.a0]
                    if s.kind in ("gv", "sv", "uv"):
                        for tt in (2 * a, 2 * a + 1):
                            dst = bank[:, (tt % 2) * 256:(tt % 2) * 256 + 256]
                            for k in range(s.kc):
                                hs = [act[:, i, k0 + k, tt * P:(tt + 1) * P] for i in (0, 1)]
                                ws = [wv[:, i, k, col0:col0 + 256] for i in (0, 1)]
                                ins = three(dst, hs, ws, k == 0, k == s.kc - 1)
                    else:
                        c0 = col0 + a * P
                        for k in range(s.kc):
                            if made and s.kind == "branch" and a == 0 and k == (KC - 1 if made.kind == "attn" else KC - 2):
                                pe.wait_ge(*finished("act", s.needs))
                                pe.wait_ge(*finished("dve", s.needs))
                            ws = [wv[:, i, k, c0:c0 + P] for i in (0, 1)]
                            hs = [act[:, i, k0 + k, 0:s.t] for i in (0, 1)]
                            ins = three(bank[:, 0:s.t], ws, hs, k == 0, k == s.kc - 1)
                    ins.then_inc(sems["product"], 1)

            def mod_columns(s, u):
                pe.wait_ge(sems["mod_copied"], u + 1)
                if u >= 2:
                    pe.wait_ge(sems["mod_reduced"], u - 1)
                for i in range(2):
                    ins = tr(w[2 + u % 2][:, i * P:(i + 1) * P], part[:, u % 2, i * P:(i + 1) * P], C["ident"])
                ins.then_inc(sems["mod_columns"], 1)

            def ada(s):
                if s.after >= 0:
                    pe.wait_ge(*finished("act", s.after))
                    pe.wait_ge(*finished("dve", s.after))
                pe.wait_ge(*arrived(s.block))
                if s.u >= 2:
                    pe.wait_ge(sems["mod_copied"], s.u - 1)
                if s.u == 1:
                    pe.wait_ge(sems["consts_in"], 32)
                    pe.wait_ge(sems["zt_ready"], 3)
                rows = w[s.u % 2]
                for r in range(2):
                    for q in range(4):
                        k = 2 * q + r
                        ins = mm(rows[32 * q:32 * q + 32, 0:256], cs[:, k, :], raw[:, s.block % NRAW, k * 256:(k + 1) * 256],
                                 start=r == 0, stop=r == 1, skip_group_check=True)
                ins.then_inc(raw_used[s.block % NRAW], 1)
                if not s.opens:
                    mod_columns(s, s.u - 1)

            def gla_part(s):
                nq = s.tq // P
                cols = slice(s.h * P, (s.h + 1) * P)
                done = s.frees if s.kind in ("gla2", "gla4") else s.needs
                pe.wait_ge(*finished("act", done))
                pe.wait_ge(*finished("dve", done))
                pe.wait_ge(*finished("pool", done))
                if s.kind == "gla1":
                    pe.wait_ge(sems["dw_in"], 16 * (s.layer + 1))
                    for d in range(2):
                        for tt in range(4):
                            ins = mm(w[d][:, tt * P:(tt + 1) * P], zt[:, tt * P:(tt + 1) * P], dw[:, d, cols], start=True, stop=True)
                        ins.then_inc(sems["gla_z"], 1)
                elif s.kind == "gla2":
                    for d in range(2):
                        for tt in range(4):
                            ins = mm(w[2 + d][:, tt * P:(tt + 1) * P], gla["la"][:, d, tt * P:(tt + 1) * P],
                                     C["tri"][:, d * P:(d + 1) * P], start=True, stop=True)
                        ins.then_inc(sems["gla_sums"], 1)
                elif s.kind == "gla3":
                    for d in range(2):
                        for tt in range(4):
                            ins = tr(w[d][:, tt * P:(tt + 1) * P], gla["ke"][:, d, tt * P:(tt + 1) * P], C["ident"])
                        ins.then_inc(sems["gla_kend_t"], 1)
                    for d in range(2):
                        for tt in range(nq):
                            c = slice(tt * P, (tt + 1) * P)
                            ins = mm(w[2 + d][:, c], gla["en"][:, d, c], gla["qd"][:, d, c], start=True, stop=True)
                        ins.then_inc(sems["gla_a"], 1)
                elif s.kind == "gla4":
                    for tt in range(nq):
                        for d in range(2):
                            mm(w[2 + tt // 2][:, (tt % 2) * 256:(tt % 2) * 256 + 256], gla["at"][:, d, tt * P:(tt + 1) * P],
                               gla["gv_s"][:, tt, :], start=(tt % 2 == 0 and d == 0), stop=False, skip_group_check=True)
                    pe.wait_ge(*finished("dve", s.needs))
                    for n in range(NCH):
                        if n < NCH - 1:
                            if n >= 2:
                                pe.wait_ge(sems["gla_state"], value("gla_state", s, 2 * (n - 1)))
                            for d in range(2):
                                c = ORDER[d][n]
                                ins = mm(w[n % 2][:, d * 256:(d + 1) * 256], gla["ktp"][:, d, c // 2, c % 2, :], gla["gv_s"][:, c // 2, :],
                                         start=True, stop=True)
                            ins.then_inc(sems["gla_u"], 1)
                        if n:
                            pe.wait_ge(sems["gla_state"], value("gla_state", s, 2 * n))
                            for d in range(2):
                                c = ORDER[d][n]
                                tt = c // 2
                                if tt < nq:
                                    ins = mm(w[2 + tt // 2][64 * (c % 2):64 * (c % 2) + 64, (tt % 2) * 256:(tt % 2) * 256 + 256],
                                             gla["qd"][:, d, chunk_cols(c)], gla["st"][:, d, n % 2, :], start=False,
                                             stop=(n == NCH - 1), skip_group_check=True)
                    ins.then_inc(sems["gla_o"], 1)
                else:
                    for c in range(2):
                        for tt in range(nq):
                            ins = tr(w[c][:, tt * P:(tt + 1) * P], o_s[:, tt, c * P:(c + 1) * P], C["ident"])
                    ins.then_inc(sems["gla_o_t"], 1)

            def attention(s):
                nq = s.tq // P
                items = [(hd, qt) for hd in s.heads for qt in range(nq)]
                probs = swa_probs if s.swa else mla_probs
                pe.wait_ge(*finished("pe", s.i - 2))
                pe.wait_ge(*finished("act", s.i - 2))
                pe.wait_ge(*finished("dve", s.i - 2))
                pe.wait_ge(*finished("pool", s.i - 2))

                def scores(i):
                    hd, qt = items[i]
                    keys = slice(0, T) if qt < 2 else slice(NLAT, T)
                    qc = slice(qt * P, (qt + 1) * P)
                    if i >= 4:
                        pe.wait_ge(sems["att_exp"], value("att_exp", s, i - 3))
                    dst = g[(i + s.bank0) % 4][:, keys]
                    if s.swa:
                        ins = mm(dst, swa["sq_s"][:, hd, qc], swa["sk_s"][:, hd // 4, keys], start=True, stop=True)
                    else:
                        mm(dst, mla["qn"][:, hd % 2, qc], mla["kn"][:, hd % 2, keys], start=True, stop=False)
                        ins = mm(dst, mla["qp"][:, qc], kpe[:, hd % 2, keys], start=False, stop=True)
                    ins.then_inc(sems["att_scores"], 1)

                def transposed(i):
                    qt = items[i][1]
                    pe.wait_ge(sems["att_p"], value("att_p", s, i + 1))
                    if i >= 2:
                        pe.wait_ge(sems["att_p_s"], value("att_p_s", s, i - 1))
                    for kt in range(0 if qt < 2 else 2, 4):
                        ins = tr(w[i % 2][:, kt * P:(kt + 1) * P], probs[i % len(probs)][:, kt * P:(kt + 1) * P], C["ident"])
                    ins.then_inc(sems["att_p_t"], 1)

                def values(i):
                    hd, qt = items[i]
                    pe.wait_ge(sems["att_p_s"], value("att_p_s", s, i + 1))
                    if qt == 0 and i >= 2 * nq:
                        pe.wait_ge(sems["att_o_s"], value("att_o_s", s, i // nq - 1))
                    pt = swa["swa_pt"][:, i % 2, :] if s.swa else mla_turned[i % 2]
                    lo = 0 if qt < 2 else 2
                    for kt in range(lo, 4):
                        v = swa["sv_s"][:, kt, (hd // 4) * P:(hd // 4 + 1) * P] if s.swa else mla["vm"][:, kt, (hd % 2) * P:(hd % 2 + 1) * P]
                        ins = mm(w[2 + hd % 2][:, qt * P:(qt + 1) * P], v, pt[:, kt * P:(kt + 1) * P], start=kt == lo, stop=kt == 3)
                    ins.then_inc(sems["att_pv"], 1)

                n = len(items)
                for i in range(-AHEAD, n + 1):
                    if i + AHEAD == 2:
                        pe.wait_ge(*finished("act", s.i - 1))
                        pe.wait_ge(*finished("dve", s.i - 1))
                    if 0 <= i + AHEAD < n:
                        scores(i + AHEAD)
                    if 0 <= i < n:
                        transposed(i)
                    if i >= 1:
                        values(i - 1)

            pe.wait_ge(sems["init_act"], 1)
            for s in steps:
                if s.kind in GEMMS:
                    product(s)
                elif s.kind == "ada":
                    ada(s)
                elif s.kind == "mod":
                    mod_columns(s, s.u)
                elif s.kind == "norm":
                    pe.wait_ge(*finished("act", s.i - 2))
                    pe.wait_ge(*finished("dve", s.i - 1))
                    pe.wait_ge(*finished("pool", s.i - 1))
                    mm(w[0][:, :s.tn], C["ones"], sums["total"][:, :s.tn], start=True, stop=False, skip_group_check=True)
                    for i in range(2):
                        pe.wait_ge(sems["norm_squares"], value("norm_squares", s, i - 1))
                        ins = mm(w[0][:, :s.tn], C["ones"], sums["sq"][:, i, :s.tn], start=False, stop=i == 1, skip_group_check=True)
                    ins.then_inc(sems["norm_sum"], 1)
                elif s.kind == "cnorm":
                    pe.wait_ge(*finished("act", s.needs))
                    pe.wait_ge(*finished("dve", s.needs))
                    for i in range(2):
                        for tt in range((s.tq if i == 0 else T) // P):
                            ins = mm(w[0][:, 4 * i + tt:4 * i + tt + 1], lat_sum[:, i, tt * P:(tt + 1) * P], C["ones"][:, 0:1], start=True, stop=True)
                    ins.then_inc(sems["lat_sum"], 1)
                    for i in range(2):
                        pe.wait_ge(sems["lat_inverse"], value("lat_inverse", s, i + 1))
                        for tt in range((s.tq if i == 0 else T) // P):
                            ins = mm(w[2 + i][:, tt * P:(tt + 1) * P], stats[:, 2, 4 * i + tt:4 * i + tt + 1].broadcast_to([P, P]), C["ident"],
                                     start=True, stop=True)
                        ins.then_inc(sems["lat_spread"], 1)
                elif s.kind[:3] == "gla":
                    gla_part(s)
                elif s.kind == "attn":
                    attention(s)

        @block.scalar
        def _(act):
            go = nc.scalar.activation
            split_next = [0]

            def round_weights(s, upto_block):
                while split_next[0] < min(upto_block + 2, len(split_blocks)) and room_for(split_next[0], s):
                    n = split_next[0]
                    b = split_blocks[n]
                    raw_n = blocks.index(b)
                    act.wait_ge(*arrived(raw_n))
                    if n >= NSPLIT:
                        act.wait_ge(*finished("pe", split_blocks[n - NSPLIT].last))
                    go(wsplit[:, n % NSPLIT, 0, :b.size], raw[:, raw_n % NRAW, :b.size], ACT.Copy).then_inc(sems["w_high"], 1)
                    split_next[0] += 1

            def evacuate(s):
                bank = [psum_g[:, 2 * s.pair + a, :] for a in range(2)]
                both = psum_g[:, 2 * s.pair:2 * s.pair + 2, :]
                names = dict(counts(s).get("act", []))
                if not names:
                    return
                act.wait_ge(*finished("act", s.i - 1))
                act.wait_ge(*finished("pe", s.after))
                act.wait_ge(*finished("dve", s.after))
                act.wait_ge(*finished("pool", s.after))
                k = s.kind
                if k in ("sq", "sk", "uqp"):
                    act.wait_ge(sems["dve_rope"], value("dve_rope", s, 5 if k != "uqp" else 2))
                    ctx_cols = slice(NLAT, T)
                    if k == "sq":
                        go(swa["sq_s"][:, 2 * s.j:2 * s.j + 2, ctx_cols], both[:, :, ctx_cols], ACT.Copy, scale=SWA_SCALE).then_inc(sems["act_evac"], 1)
                    elif k == "sk":
                        go(swa["sk_s"][:, :, ctx_cols], both[:, :, ctx_cols], ACT.Copy).then_inc(sems["act_evac"], 1)
                    else:
                        go(mla["qp"][:, ctx_cols], bank[0][:, ctx_cols], ACT.Copy, scale=MLA_SCALE).then_inc(sems["act_evac"], 1)
                    return
                act.wait_ge(sems["product"], value("product", s, 1))
                if k == "zk":
                    go(zt[0:32, :], bank[0][0:32, :], ACT.Copy).then_inc(sems["act_evac"], 1)
                elif k == "gq":
                    go(gla["gq_s"][:, s.j % 2, :s.t], bank[0][:, :s.t], ACT.Copy, scale=GLA_DK ** -0.5).then_inc(sems["act_evac"], 1)
                elif k in ("gv", "sv", "uv"):
                    dst = {"gv": gla["gv_s"], "sv": swa["sv_s"], "uv": mla["vm"]}[k]
                    go(dst[:, 0:2, :], bank[0].rearrange("p (t n) -> p t n", n=256), ACT.Copy).then_inc(sems["act_evac"], 1)
                elif k == "gr":
                    go(gla["gr_s"][:, s.a0, :s.t], bank[0][:, :s.t], ACT.Silu).then_inc(sems["act_evac"], 1)
                elif k == "cq":
                    dst = lat["cx"][:, (0, 3, 2)[s.j], :s.t]
                    go(dst, bank[0][:, :s.t], ACT.Copy).then_inc(sems["act_evac"], 1)
                elif k == "ukn":
                    go(mla["kn"][:, 0, :], bank[0], ACT.Copy).then_inc(sems["act_evac"], 1)
                elif k == "uqn":
                    go(mla["qn"][:, 0, :s.t], bank[0][:, :s.t], ACT.Copy, scale=MLA_SCALE).then_inc(sems["act_evac"], 1)
                elif k == "gate":
                    for a in range(2):
                        act.wait_ge(sems["product"], value("product", s, a + 1))
                        go(br["sg"][:, s.j % 2, a, :s.t], bank[a][:, :s.t], ACT.Sigmoid).then_inc(sems["act_evac"], 1)
                elif k == "up":
                    act.wait_ge(sems["product"], value("product", s, 2))
                    go(ups["rt"][:, s.j % 2, :, :s.t], both[:, :, :s.t], ACT.Relu).then_inc(sems["act_evac"], 1)
                    act.wait_ge(sems["act_evac"], value("act_evac", s, 1))
                    go(hid[s.q % 2][:, 0, 2 * s.j:2 * s.j + 2, :s.t], ups["rt"][:, s.j % 2, :, :s.t], ACT.Square).then_inc(sems["up_high"], 1)

            def gla_part(s):
                nq = s.tq // P
                act.wait_ge(*finished("act", s.i - 1))
                done = s.frees if s.kind == "gla2" else s.needs
                act.wait_ge(*finished("pe", done))
                act.wait_ge(*finished("dve", done))
                act.wait_ge(*finished("pool", done))
                if s.kind == "gla1":
                    for d in range(2):
                        act.wait_ge(sems["gla_z"], value("gla_z", s, d + 1))
                        go(gla["la"][:, d, :], psum_w[:, d, :], ACT.Abs).then_inc(sems["gla_abs"], 1)
                    act.wait_ge(sems["gla_abs"], value("gla_abs", s, 2))
                    go(gla["la"][:, :, :], gla["la"][:, :, :], ACT.Exp, scale=-1.0).then_inc(sems["gla_exp_z"], 1)
                    act.wait_ge(sems["gla_exp_z"], value("gla_exp_z", s, 1))
                    for d in range(2):
                        go(gla["la"][:, d, :], gla["la"][:, d, :], ACT.Ln, bias=1.0).then_inc(sems["gla_ln"], 1)
                elif s.kind == "gla2":
                    for d in range(2):
                        act.wait_ge(sems["gla_sums"], value("gla_sums", s, d + 1))
                        go(gla["ep"][:, d, :], psum_w[:, 2 + d, :], ACT.Exp).then_inc(sems["gla_exps"], 1)
                        go(gla["en"][:, d, :], psum_w[:, 2 + d, :], ACT.Exp, scale=-1.0).then_inc(sems["gla_exps"], 1)
                    for d in range(2):
                        act.wait_ge(sems["gla_to_end"], value("gla_to_end", s, d + 1))
                        go(gla["ke"][:, d, :], gla["ke"][:, d, :], ACT.Exp).then_inc(sems["gla_exp_end"], 1)
                elif s.kind == "gla3":
                    for d in range(2):
                        act.wait_ge(sems["gla_kend_t"], value("gla_kend_t", s, d + 1))
                        for a in range(2):
                            rows = slice(64 * a, 64 * a + 64)
                            go(gla["ktp"][rows, d, :, a, :], psum_w[rows, d, :].rearrange("p (t n) -> p t n", n=P), ACT.Copy)\
                                .then_inc(sems["gla_kend_s"], 1)
                elif s.kind == "gla4":
                    go(spare[:], tiny[:], ACT.Sqrt).then_inc(sems["table"], 1)
                    act.wait_ge(sems["gla_o"], value("gla_o", s, 1))
                    for tt in range(nq):
                        src = psum_w[:, 2 + tt // 2, (tt % 2) * 256:(tt % 2) * 256 + 256]
                        go(gla["en"][:, tt // 2, (tt % 2) * 256:(tt % 2) * 256 + 256], src, ACT.Square,
                           accum_out=stats[:, 0, tt:tt + 1]).then_inc(sems["gla_sumsq"], 1)
                    act.wait_ge(sems["gla_sumsq"], value("gla_sumsq", s, nq))
                    go(stats[:, 1, 0:nq], stats[:, 0, 0:nq], ACT.Sqrt, scale=1.0 / GLA_DV, bias=tiny[:, 0:1]).then_inc(sems["gla_root"], 1)
                else:
                    for c in range(2):
                        act.wait_ge(sems["gla_out"], value("gla_out", s, c + 1))
                        go(osplit[:, 0, 2 * s.h + c, :s.tq], gla["ke"][:, c, :s.tq], ACT.Copy).then_inc(sems["gla_high"], 1)

            def attention(s):
                nq = s.tq // P
                n = len(s.heads) * nq
                probs = swa_probs if s.swa else mla_probs
                oc = swa["swa_o"] if s.swa else mla_o
                act.wait_ge(*finished("pe", s.i - 1))
                act.wait_ge(*finished("act", s.i - 1))
                act.wait_ge(*finished("dve", s.i - 1))
                act.wait_ge(*finished("pool", s.i - 1))

                def exponentials(i):
                    keys = slice(0, T) if i % nq < 2 else slice(NLAT, T)
                    if s.swa:
                        act.wait_ge(sems["att_sunk"], value("att_sunk", s, i + 1))
                    else:
                        act.wait_ge(sems["att_max"], value("att_max", s, i + 1))
                    if i >= len(probs):
                        act.wait_ge(sems["att_p_t"], value("att_p_t", s, i + 1 - len(probs)))
                    go(probs[i % len(probs)][:, keys], psum_g[:, (i + s.bank0) % 4, keys], ACT.Exp, bias=stats[:, 1 if s.swa else 0, i:i + 1],
                       accum_out=stats[:, 2, i:i + 1]).then_inc(sems["att_exp"], 1)
                    if s.swa:
                        hd = s.heads[i // nq]
                        go(stats[:, 3, i:i + 1], stats[:, 1, i:i + 1], ACT.Exp, bias=vec[:, VEC["sink", s.layer]][:, hd:hd + 1])\
                            .then_inc(sems["att_exp_sink"], 1)

                def copied(i):
                    keys = slice(0, T) if i % nq < 2 else slice(NLAT, T)
                    act.wait_ge(sems["att_p_t"], value("att_p_t", s, i + 1))
                    pt = swa["swa_pt"][:, i % 2, :] if s.swa else mla_turned[i % 2]
                    go(pt[:, keys], psum_w[:, i % 2, keys], ACT.Copy).then_inc(sems["att_p_s"], 1)

                def head_out(hh):
                    act.wait_ge(sems["att_pv"], value("att_pv", s, nq * (hh + 1)))
                    if hh:
                        act.wait_ge(sems["att_low"], value("att_low", s, hh))
                    go(oc[:, :s.tq], psum_w[:, 2 + hh % 2, :s.tq], ACT.Copy).then_inc(sems["att_o_s"], 1)
                    act.wait_ge(sems["att_o_s"], value("att_o_s", s, hh + 1))
                    go(osplit[:, 0, s.heads[hh], :s.tq], oc[:, :s.tq], ACT.Copy).then_inc(sems["att_high"], 1)

                for i in range(n + 1):
                    if i < n:
                        exponentials(i)
                    if i >= 1:
                        copied(i - 1)
                    if i > nq and i % nq == 1:
                        head_out(i // nq - 1)
                head_out(len(s.heads) - 1)

            act.wait_ge(sems["cvec_in"], 16)
            go(cs[:], cs[:], ACT.Silu).then_inc(sems["init_act"], 1)
            act.wait_ge(sems["init_dve"], 1)
            next_split = -1
            for s in steps:
                if s.block is not None and blocks[s.block].split:
                    next_split = max(next_split, split_of[id(blocks[s.block])])
                round_weights(s, next_split if s.i > opening else -2)
                if s.kind in GEMMS:
                    evacuate(s)
                elif s.kind == "ada":
                    if s.u:
                        act.wait_ge(*finished("act", s.i - 1))
                    if s.u == 1:
                        act.dma_start(x[:], xt).then_inc(sems["x_in"], 16)
                    act.wait_ge(*used(s.block))
                    if s.u >= 2:
                        act.wait_ge(sems["mod_columns"], s.u - 1)
                    go(part[:, s.u % 2, :], psum_w[:, s.u % 2, 0:256], ACT.Copy).then_inc(sems["mod_copied"], 1)
                elif s.kind == "norm":
                    act.wait_ge(*finished("pe", s.i - 1))
                    act.wait_ge(*finished("act", s.i - 1))
                    act.wait_ge(*finished("dve", s.i - 1))
                    act.wait_ge(*finished("pool", s.i - 1))
                    if s.which == "mix":
                        act.dma_start(dw[:], decay_w[s.layer]).then_inc(sems["dw_in"], 16)
                    go(spare[:], tiny[:], ACT.Sqrt).then_inc(sems["table"], 1)
                    act.wait_ge(sems["norm_sum"], value("norm_sum", s, 1))
                    go(nrm["root"][:, :s.tn], psum_w[:, 0, :s.tn], ACT.Sqrt, scale=1.0 / D, bias=tiny[:, 0:1]).then_inc(sems["norm_root"], 1)
                    if s.which != "final":
                        m = {"mix": 0, "mlp": 1}[s.which]
                        for c in range(KC):
                            if c % 2:
                                act.wait_ge(sems["norm_scaled_odd"], value("norm_scaled_odd", s, c // 2 + 1))
                            else:
                                act.wait_ge(sems["norm_scaled"], value("norm_scaled", s, c // 2 + 1))
                            for r in range(s.tn // NLAT):
                                cols = slice(r * NLAT, (r + 1) * NLAT)
                                ins = go(nrm["xn"][:, c, cols], nrm["xn"][:, c, cols], ACT.Identity, scale=gain[:, s.layer, m, c, r:r + 1],
                                         bias=mod[:, s.layer, 3 * KC * m + c, r:r + 1])
                            ins.then_inc(sems["norm_shifted"], 1)
                            if c % 2:
                                act.wait_ge(sems["norm_shifted"], value("norm_shifted", s, c + 1))
                                go(hsplit[:, 0, c, :s.tn], nrm["xn"][:, c, :s.tn], ACT.Copy).then_inc(sems["norm_high_odd"], 1)
                elif s.kind == "squares" and s.j == 3:
                    act.wait_ge(sems["x_in"], 16)
                    act.wait_ge(*finished("act", s.i - 1))
                    act.wait_ge(*finished("dve", s.after))
                    for i in range(2):
                        go(sums["sq"][:, i, :s.tn], x[:, 2 * s.j + i, :s.tn], ACT.Square).then_inc(sems["norm_squares"], 1)
                elif s.kind == "csum":
                    act.wait_ge(*finished("act", s.i - 1))
                    act.wait_ge(*finished("dve", s.i - 1))
                    for a, b, tn in ((0, 3, s.tq), (3, 5, T)):
                        go(lat["cx_sq"][:, a:b, :tn], lat["cx"][:, a:b, :tn], ACT.Square).then_inc(sems["lat_squares"], 1)
                elif s.kind == "cnorm":
                    act.wait_ge(*finished("act", s.i - 1))
                    act.wait_ge(*finished("dve", s.needs))
                    go(spare[:], tiny[:], ACT.Sqrt).then_inc(sems["table"], 1)
                    act.wait_ge(sems["lat_sum"], value("lat_sum", s, 1))
                    for i, (a, b, tn) in enumerate(((0, 3, s.tq), (3, 5, T))):
                        cols = slice(4 * i, 4 * i + tn // P)
                        go(stats[:, 1, cols], psum_w[:, 0, cols], ACT.Sqrt, scale=1.0 / (P * (b - a)), bias=tiny[:, 0:1]).then_inc(sems["lat_root"], 1)
                    act.wait_ge(*finished("pe", s.i - 1))
                    act.wait_ge(*finished("dve", s.i - 1))
                    act.wait_ge(*finished("pool", s.i - 1))
                    for c in range(5):
                        tn = s.tq if c < 3 else T
                        act.wait_ge(sems["lat_scaled"], value("lat_scaled", s, c + 1))
                        go(mla["cn_r"][:, 0, c, :tn], lat["cx"][:, c, :tn], ACT.Copy).then_inc(sems["lat_high"], 1)
                    round_weights(s, next_split + 1)
                elif s.kind == "krope":
                    act.wait_ge(*finished("act", s.i - 1))
                    act.wait_ge(*finished("pe", s.i - 2))
                    act.wait_ge(*finished("dve", s.i - 2))
                    for a in range(2):
                        rows = slice(64 * a, 64 * a + 64)
                        go(kpe[rows, a, NLAT:T], kr[rows, NLAT:T], ACT.Copy).then_inc(sems["lat_kr"], 1)
                elif s.kind == "merge":
                    act.wait_ge(*finished("act", s.i - 1))
                    act.wait_ge(*finished("pe", s.after))
                    act.wait_ge(*finished("pool", s.needs))
                    for c in (2 * s.j, 2 * s.j + 1):
                        go(hsplit[:, 0, c, :s.tq], mg[:, c, :s.tq], ACT.Copy).then_inc(sems["merge_high"], 1)
                elif s.kind[:3] == "gla":
                    gla_part(s)
                elif s.kind == "attn":
                    attention(s)
                    round_weights(s, next_split + 1)

        @block.vector
        def _(dve):
            v = nc.vector
            split_next = [0]

            def split_weights(s, upto_block):
                while split_next[0] < min(upto_block + 2, len(split_blocks)) and room_for(split_next[0], s):
                    n = split_next[0]
                    b = split_blocks[n]
                    raw_n = blocks.index(b)
                    dve.wait_ge(sems["w_high"], n + 1)
                    v.tensor_tensor(wsplit[:, n % NSPLIT, 1, :b.size], raw[:, raw_n % NRAW, :b.size],
                                    wsplit[:, n % NSPLIT, 0, :b.size].bitcast(F32), ALU.subtract).then_inc(raw_used[raw_n % NRAW], 1)
                    split_next[0] += 1

            def rope(s):
                both = psum_g[:, 2 * s.pair:2 * s.pair + 2, 0:NLAT]
                scale = SWA_SCALE if s.kind == "sq" else 1.0
                dve.wait_ge(sems["product"], value("product", s, 2))
                cos = C["swa_cos"].unsqueeze(1).broadcast_to([P, 2, NLAT])
                v.scalar_tensor_tensor(swa["rp"][:, 0], both, scale, cos, ALU.mult, ALU.mult).then_inc(sems["dve_rope"], 1)
                for a in range(4):
                    b = a ^ 1
                    src, dst = slice(32 * b, 32 * b + 32), slice(32 * a, 32 * a + 32)
                    sin = cst[src, CONST["swa_sin"]].unsqueeze(1).broadcast_to([32, 2, NLAT])
                    v.scalar_tensor_tensor(swa["rp"][dst, 1], psum_g[src, 2 * s.pair:2 * s.pair + 2, 0:NLAT], scale, sin,
                                           ALU.mult, ALU.mult).then_inc(sems["dve_rope"], 1)

            def evacuate(s):
                bank = [psum_g[:, 2 * s.pair + a, :] for a in range(2)]
                both = psum_g[:, 2 * s.pair:2 * s.pair + 2, :]
                if "dve" not in counts(s):
                    return
                dve.wait_ge(*finished("dve", s.i - 1))
                dve.wait_ge(*finished("pe", s.after))
                dve.wait_ge(*finished("act", s.after))
                dve.wait_ge(*finished("pool", s.after))
                k = s.kind
                if k in ("sq", "sk"):
                    rope(s)
                    return
                if k == "uqp":
                    dve.wait_ge(sems["product"], value("product", s, 1))
                    v.scalar_tensor_tensor(mla["mla_p"][:, 0, 0:NLAT], bank[0][:, 0:NLAT], MLA_SCALE, C["mla_cos"], ALU.mult, ALU.mult).then_inc(sems["dve_rope"], 1)
                    v.stream_shuffle(mla["mla_p"][:, 1, 0:NLAT], bank[0][:, 0:NLAT], [(r + 16) % 32 for r in range(32)]).then_inc(sems["dve_rope"], 1)
                    dve.wait_ge(sems["dve_rope"], value("dve_rope", s, 2))
                    v.scalar_tensor_tensor(mla["mla_p"][:, 1, 0:NLAT], mla["mla_p"][:, 1, 0:NLAT], MLA_SCALE, C["mla_sin"], ALU.mult, ALU.mult).then_inc(sems["dve_rope"], 1)
                    return
                dve.wait_ge(sems["product"], value("product", s, s.tiles))
                if k == "zk":
                    v.tensor_copy(kr[:], bank[1]).then_inc(sems["dve_evac"], 1)
                elif k == "gk":
                    v.tensor_copy(gla["gk_s"][:, s.j % 2, :], bank[0]).then_inc(sems["dve_evac"], 1)
                elif k in ("gv", "sv", "uv"):
                    dst = {"gv": gla["gv_s"], "sv": swa["sv_s"], "uv": mla["vm"]}[k]
                    v.tensor_copy(dst[:, 2:4, :], bank[s.tiles - 1].rearrange("p (t n) -> p t n", n=256)).then_inc(sems["dve_evac"], 1)
                elif k == "cq":
                    v.tensor_copy(lat["cx"][:, (1, 4)[s.j], :s.t], bank[1][:, :s.t]).then_inc(sems["dve_evac"], 1)
                elif k == "ukn":
                    v.tensor_copy(mla["kn"][:, 1, :], bank[1]).then_inc(sems["dve_evac"], 1)
                elif k == "uqn":
                    v.tensor_scalar(mla["qn"][:, 1, :s.t], bank[1][:, :s.t], MLA_SCALE, None, ALU.mult).then_inc(sems["dve_evac"], 1)
                elif k == "branch":
                    dve.wait_ge(*finished("act", s.i - 1))
                    dst = mg[:, 2 * s.j:2 * s.j + 2, :s.t] if s.branch == 0 else br["bt"][:, s.j % 2, :, :s.t]
                    v.tensor_tensor(dst, both[:, :, :s.t], br["sg"][:, s.j % 2, :, :s.t], ALU.mult).then_inc(sems["dve_evac"], 1)
                elif k == "up":
                    dve.wait_ge(sems["act_evac"], value("act_evac", s, 1))
                    r = ups["rt"][:, s.j % 2, :, :s.t]
                    v.tensor_tensor(ups["rt_sq"][:, s.j % 2, :, :s.t], r, r, ALU.mult).then_inc(sems["dve_evac"], 1)
                    dve.wait_ge(sems["dve_evac"], value("dve_evac", s, 1))
                    dve.wait_ge(sems["up_high"], value("up_high", s, 1))
                    v.tensor_tensor(hid[s.q % 2][:, 1, 2 * s.j:2 * s.j + 2, :s.t], ups["rt_sq"][:, s.j % 2, :, :s.t],
                                    hid[s.q % 2][:, 0, 2 * s.j:2 * s.j + 2, :s.t].bitcast(F32), ALU.subtract).then_inc(sems["up_low"], 1)
                else:
                    m = 2 if k == "out" else 5
                    for a in range(2):
                        for r in range(s.t // NLAT):
                            c, cols = 2 * s.j + a, slice(r * NLAT, (r + 1) * NLAT)
                            v.scalar_tensor_tensor(x[:, c, cols], bank[a][:, cols], mod[:, s.layer, m * KC + c, r:r + 1], x[:, c, cols],
                                                   ALU.mult, ALU.add).then_inc(sems["dve_evac"], 1)

            def reduce_columns(s, u):
                dve.wait_ge(*finished("dve", s.i - 1))
                dve.wait_ge(sems["mod_columns"], value("mod_columns", s, 1))
                l, j = u // 24, u % 24
                src = psum_w[:, 2 + u % 2, 0:256].rearrange("p (t q n) -> p t n q", t=2, q=4)[:, :, 0:2, :]
                v.tensor_reduce(mod[:, l, 2 * j:2 * j + 2, :], src, AX.X, ALU.add).then_inc(sems["mod_reduced"], 1)

            def gla_part(s):
                nq = s.tq // P
                h2 = s.h % 2
                dve.wait_ge(*finished("dve", s.i - 1))
                dve.wait_ge(*finished("pe", s.needs))
                dve.wait_ge(*finished("act", s.needs))
                dve.wait_ge(*finished("pool", s.needs))
                if s.kind == "gla1":
                    for d in range(2):
                        dve.wait_ge(sems["gla_ln"], value("gla_ln", s, d + 1))
                        v.scalar_tensor_tensor(gla["la"][:, d, :], psum_w[:, d, :], 0.0, gla["la"][:, d, :], ALU.min, ALU.subtract)\
                            .then_inc(sems["gla_la"], 1)
                elif s.kind == "gla2":
                    for d in range(2):
                        dve.wait_ge(sems["gla_exps"], value("gla_exps", s, 2 * (d + 1)))
                        sums = psum_w[:, 2 + d, :].rearrange("p (c n) -> p c n", n=GLA_CHUNK)
                        v.tensor_copy(gla["last"][:, d, :], sums[:, :, last_col(d, 0)]).then_inc(sems["gla_last"], 1)
                        dve.wait_ge(sems["gla_last"], value("gla_last", s, d + 1))
                        v.tensor_tensor(gla["ke"][:, d, :].rearrange("p (c n) -> p c n", n=GLA_CHUNK),
                                        gla["last"][:, d, :].unsqueeze(2).broadcast_to([P, NCH, GLA_CHUNK]), sums, ALU.subtract)\
                            .then_inc(sems["gla_to_end"], 1)
                    for d in range(2):
                        v.tensor_tensor(gla["en"][:, d, :], gla["gk_s"][:, h2, :], gla["en"][:, d, :], ALU.mult).then_inc(sems["gla_kinv"], 1)
                elif s.kind == "gla3":
                    for d in range(2):
                        dve.wait_ge(sems["gla_a"], value("gla_a", s, d + 1))
                        mask = C["tri"][:, d * P:(d + 1) * P].bitcast(U32).unsqueeze(1).broadcast_to([P, nq, P])
                        v.copy_predicated(gla["at"][:, d, :s.tq].rearrange("p (t n) -> p t n", n=P), mask,
                                          psum_w[:, 2 + d, :s.tq].rearrange("p (t n) -> p t n", n=P)).then_inc(sems["gla_masked"], 1)
                elif s.kind == "gla4":
                    for n in range(NCH - 1):
                        dve.wait_ge(sems["gla_u"], value("gla_u", s, n + 1))
                        for d in range(2):
                            c = ORDER[d][n]
                            u = psum_w[:, n % 2, d * 256:(d + 1) * 256]
                            if n == 0:
                                v.tensor_copy(gla["st"][:, d, 1, :], u).then_inc(sems["gla_state"], 1)
                            else:
                                dve.wait_ge(sems["gla_state"], value("gla_state", s, 2 * n - 1 + d))
                                v.scalar_tensor_tensor(gla["st"][:, d, (n + 1) % 2, :], gla["st"][:, d, n % 2, :],
                                                       gla["ep"][:, d, last_col(d, c):last_col(d, c) + 1], u, ALU.mult, ALU.add)\
                                    .then_inc(sems["gla_state"], 1)
                    dve.wait_ge(sems["gla_root"], value("gla_root", s, 1))
                    v.reciprocal(stats[:, 2, 0:nq], stats[:, 1, 0:nq]).then_inc(sems["gla_inverse"], 1)
                    dve.wait_ge(sems["gla_inverse"], value("gla_inverse", s, 1))
                    for tt in range(nq):
                        v.tensor_scalar(o_s[:, tt, :], psum_w[:, 2 + tt // 2, (tt % 2) * 256:(tt % 2) * 256 + 256],
                                        stats[:, 2, tt:tt + 1], None, ALU.mult).then_inc(sems["gla_o_s"], 1)
                else:
                    dve.wait_ge(sems["gla_o_t"], value("gla_o_t", s, 1))
                    for c in range(2):
                        v.scalar_tensor_tensor(gla["ke"][:, c, :s.tq], psum_w[:, c, :s.tq], vec[:, VEC["gla", s.layer]][:, c:c + 1],
                                               gla["gr_s"][:, c, :s.tq], ALU.mult, ALU.mult).then_inc(sems["gla_out"], 1)
                    for c in range(2):
                        dve.wait_ge(sems["gla_high"], value("gla_high", s, c + 1))
                        v.tensor_tensor(osplit[:, 1, 2 * s.h + c, :s.tq], gla["ke"][:, c, :s.tq],
                                        osplit[:, 0, 2 * s.h + c, :s.tq].bitcast(F32), ALU.subtract).then_inc(sems["gla_low"], 1)

            def attention(s):
                nq = s.tq // P
                n = len(s.heads) * nq
                probs = swa_probs if s.swa else mla_probs
                oc = swa["swa_o"] if s.swa else mla_o
                masked = [0]
                dve.wait_ge(*finished("pe", s.i - 1))
                dve.wait_ge(*finished("act", s.i - 1))
                dve.wait_ge(*finished("dve", s.i - 1))
                dve.wait_ge(*finished("pool", s.i - 1))

                def maximum(i):
                    qt = i % nq
                    keys = slice(0, T) if qt < 2 else slice(NLAT, T)
                    dve.wait_ge(sems["att_scores"], value("att_scores", s, i + 1))
                    if s.swa and qt < 2:
                        far = psum_g[:, (i + s.bank0) % 4, P * (1 - qt):P * (2 - qt)]
                        v.tensor_tensor(far, far, C["band"][:, qt * P:(qt + 1) * P], ALU.add).then_inc(sems["att_masked"], 1)
                        masked[0] += 1
                        dve.wait_ge(sems["att_masked"], value("att_masked", s, masked[0]))
                    v.tensor_reduce(stats[:, 0, i:i + 1], psum_g[:, (i + s.bank0) % 4, keys], AX.X, ALU.max, negate=True).then_inc(sems["att_max"], 1)

                def with_sink(i):
                    hd = s.heads[i // nq]
                    dve.wait_ge(sems["att_max"], value("att_max", s, i + 1))
                    v.tensor_scalar(stats[:, 1, i:i + 1], stats[:, 0, i:i + 1], nsink[:, s.layer, hd:hd + 1], None, ALU.min)\
                        .then_inc(sems["att_sunk"], 1)

                def total_with_sink(i):
                    dve.wait_ge(sems["att_exp"], value("att_exp", s, i + 1))
                    dve.wait_ge(sems["att_exp_sink"], value("att_exp_sink", s, i + 1))
                    v.tensor_tensor(stats[:, 4, i:i + 1], stats[:, 2, i:i + 1], stats[:, 3, i:i + 1], ALU.add).then_inc(sems["att_total"], 1)

                def normalise(i):
                    keys = slice(0, T) if i % nq < 2 else slice(NLAT, T)
                    if s.swa:
                        dve.wait_ge(sems["att_total"], value("att_total", s, i + 1))
                        total = stats[:, 4, i:i + 1]
                    else:
                        dve.wait_ge(sems["att_exp"], value("att_exp", s, i + 1))
                        total = stats[:, 2, i:i + 1]
                    v.reciprocal(stats[:, 5, i:i + 1], total).then_inc(sems["att_inverse"], 1)
                    dve.wait_ge(sems["att_inverse"], value("att_inverse", s, i + 1))
                    v.tensor_scalar(probs[i % len(probs)][:, keys], probs[i % len(probs)][:, keys], stats[:, 5, i:i + 1], None, ALU.mult).then_inc(sems["att_p"], 1)

                def low(hh):
                    dve.wait_ge(sems["att_high"], value("att_high", s, hh + 1))
                    v.tensor_tensor(osplit[:, 1, s.heads[hh], :s.tq], oc[:, :s.tq], osplit[:, 0, s.heads[hh], :s.tq].bitcast(F32),
                                    ALU.subtract).then_inc(sems["att_low"], 1)

                for i in range(n + 1):
                    if i < n:
                        maximum(i)
                    if i and s.swa:
                        total_with_sink(i - 1)
                    if i < n and s.swa:
                        with_sink(i)
                    if i:
                        normalise(i - 1)
                    if n > i >= nq + 2 and (i - 2) % nq == 0:
                        low((i - 2) // nq - 1)
                for hh in range((n - 3) // nq, len(s.heads)):
                    low(hh)

            dve.wait_ge(sems["consts_in"], 32)
            v.memset(tiny[:], EPS).then_inc(sems["init_dve"], 1)
            for l in range(DEPTH):
                v.tensor_scalar(nsink[:, l, :], vec[:, VEC["sink", l]], -1.0, None, ALU.mult).then_inc(sems["init_dve"], 1)
            dve.wait_ge(sems["init_dve"], 3)
            next_split = -1
            for s in steps:
                if s.block is not None and blocks[s.block].split:
                    next_split = max(next_split, split_of[id(blocks[s.block])])
                split_weights(s, next_split if s.i > opening else -2)
                if s.kind in GEMMS:
                    evacuate(s)
                elif s.kind == "ada":
                    if not s.opens:
                        reduce_columns(s, s.u - 1)
                elif s.kind == "mod":
                    l = s.layer
                    reduce_columns(s, s.u)
                    dve.wait_ge(sems["mod_reduced"], value("mod_reduced", s, 1))
                    new = (slice(0, 2 * KC), slice(2 * KC, 6 * KC), slice(0, 6 * KC))[s.q]
                    bias = vec[:, VEC["ada_b", l]][:, new]
                    v.tensor_tensor(mod[:, l, new], mod[:, l, new], bias.unsqueeze(2).broadcast_to([P, new.stop - new.start, 2]), ALU.add)\
                        .then_inc(sems["mod_final"], 1)
                    dve.wait_ge(sems["mod_final"], value("mod_final", s, 1))
                    for m, name in ((0, "mix"), (1, "mlp")):
                        if s.q in (m, 2):
                            first = (3 * m + 1) * KC
                            v.scalar_tensor_tensor(gain[:, l, m], mod[:, l, first:first + KC, :], 1.0,
                                                   vec[:, VEC[name, l]].unsqueeze(2).broadcast_to([P, KC, 2]), ALU.add, ALU.mult)\
                                .then_inc(sems["mod_final"], 1)
                elif s.kind == "norm":
                    dve.wait_ge(*finished("pe", s.i - 1))
                    dve.wait_ge(*finished("act", s.i - 1))
                    dve.wait_ge(*finished("dve", s.i - 1))
                    dve.wait_ge(*finished("pool", s.i - 1))
                    dve.wait_ge(sems["norm_root"], value("norm_root", s, 1))
                    v.reciprocal(nrm["rinv"][:, :s.tn], nrm["root"][:, :s.tn]).then_inc(sems["norm_inverse"], 1)
                    dve.wait_ge(sems["norm_inverse"], value("norm_inverse", s, 1))
                    if s.which == "final":
                        for c in range(KC):
                            v.scalar_tensor_tensor(nrm["xn"][:, c, :s.tn], x[:, c, :s.tn], vec[:, VEC["final", 0]][:, c:c + 1],
                                                   nrm["rinv"][:, :s.tn], ALU.mult, ALU.mult).then_inc(sems["norm_scaled"], 1)
                        continue
                    v.tensor_tensor(nrm["xn"][:, 0, :s.tn], x[:, 0, :s.tn], nrm["rinv"][:, :s.tn], ALU.mult).then_inc(sems["norm_scaled"], 1)
                    for c in range(KC):
                        if c % 2 == 0:
                            if c + 2 < KC:
                                v.tensor_tensor(nrm["xn"][:, c + 2, :s.tn], x[:, c + 2, :s.tn], nrm["rinv"][:, :s.tn], ALU.mult)\
                                    .then_inc(sems["norm_scaled"], 1)
                            dve.wait_ge(sems["norm_shifted"], value("norm_shifted", s, c + 1))
                            v.tensor_copy(hsplit[:, 0, c, :s.tn], nrm["xn"][:, c, :s.tn]).then_inc(sems["norm_high"], 1)
                            dve.wait_ge(sems["norm_high"], value("norm_high", s, c // 2 + 1))
                        else:
                            dve.wait_ge(sems["norm_high_odd"], value("norm_high_odd", s, c // 2 + 1))
                        v.tensor_tensor(hsplit[:, 1, c, :s.tn], nrm["xn"][:, c, :s.tn], hsplit[:, 0, c, :s.tn].bitcast(F32), ALU.subtract)\
                            .then_inc(sems["norm_low"], 1)
                elif s.kind == "csum":
                    dve.wait_ge(*finished("dve", s.i - 1))
                    for i, (a, b, tn) in enumerate(((0, 3, s.tq), (3, 5, T))):
                        dve.wait_ge(sems["lat_squares"], value("lat_squares", s, i + 1))
                        v.tensor_reduce(lat_sum[:, i, :tn], lat["cx_sq"][:, a:b, :tn].rearrange("p c t -> p t c"), AX.X, ALU.add).then_inc(sems["lat_reduced"], 1)
                elif s.kind == "cnorm":
                    dve.wait_ge(*finished("dve", s.i - 1))
                    for i, tn in ((0, s.tq), (1, T)):
                        cols = slice(4 * i, 4 * i + tn // P)
                        dve.wait_ge(sems["lat_root"], value("lat_root", s, i + 1))
                        v.reciprocal(stats[:, 2, cols], stats[:, 1, cols]).then_inc(sems["lat_inverse"], 1)
                    for i, chunks, tn in ((0, range(0, 3), s.tq), (1, range(3, 5), T)):
                        dve.wait_ge(sems["lat_spread"], value("lat_spread", s, i + 1))
                        for c in range(chunks[0], chunks[-1] + 2):
                            if c in chunks:
                                wc = vec[:, VEC["mkv" if i else "mq", s.layer]][:, c - chunks[0]:c - chunks[0] + 1]
                                v.scalar_tensor_tensor(lat["cx"][:, c, :tn], lat["cx"][:, c, :tn], wc, psum_w[:, 2 + i, :tn], ALU.mult, ALU.mult)\
                                    .then_inc(sems["lat_scaled"], 1)
                            if c - 1 in chunks:
                                dve.wait_ge(sems["lat_high"], value("lat_high", s, c))
                                v.tensor_tensor(mla["cn_r"][:, 1, c - 1, :tn], lat["cx"][:, c - 1, :tn], mla["cn_r"][:, 0, c - 1, :tn].bitcast(F32),
                                                ALU.subtract).then_inc(sems["lat_low"], 1)
                    split_weights(s, next_split + 1)
                elif s.kind == "krope":
                    dve.wait_ge(*finished("dve", s.i - 1))
                    dve.wait_ge(*finished("act", s.i - 2))
                    v.tensor_tensor(lat["cx_sq"][:, 2, 0:NLAT], kr[:, 0:NLAT], C["mla_cos"], ALU.mult).then_inc(sems["lat_rope"], 1)
                    v.stream_shuffle(lat["cx_sq"][:, 3, 0:NLAT], kr[:, 0:NLAT], [(r + 16) % 32 for r in range(32)]).then_inc(sems["lat_rope"], 1)
                    dve.wait_ge(sems["lat_rope"], value("lat_rope", s, 2))
                    v.tensor_tensor(lat["cx_sq"][:, 3, 0:NLAT], lat["cx_sq"][:, 3, 0:NLAT], C["mla_sin"], ALU.mult).then_inc(sems["lat_rope"], 1)
                elif s.kind == "merge":
                    dve.wait_ge(*finished("dve", s.i - 1))
                    dve.wait_ge(*finished("pe", s.after))
                    dve.wait_ge(*finished("pool", s.needs))
                    for i in range(2):
                        c = 2 * s.j + i
                        dve.wait_ge(sems["merge_high"], value("merge_high", s, i + 1))
                        v.tensor_tensor(hsplit[:, 1, c, :s.tq], mg[:, c, :s.tq], hsplit[:, 0, c, :s.tq].bitcast(F32), ALU.subtract).then_inc(sems["merge_low"], 1)
                elif s.kind[:3] == "gla":
                    gla_part(s)
                elif s.kind == "attn":
                    attention(s)
                    split_weights(s, next_split + 1)

        @block.gpsimd
        def _(pool):
            gp = nc.gpsimd
            for rows in (slice(32, 64), slice(64, 128)):
                gp.memset(zt[rows, :], 0.0).then_inc(sems["zt_ready"], 1)
            pool.wait_ge(sems["zt_ready"], 2)
            gp.memset(zt[32:33, :], 1.0).then_inc(sems["zt_ready"], 1)
            pool.wait_ge(sems["zt_ready"], 3)
            for s in steps:
                if not counts(s).get("pool"):
                    continue
                k = s.kind
                pool.wait_ge(*finished("pool", s.i - 1))
                if k in GEMMS:
                    pool.wait_ge(*finished("pe", s.after))
                    pool.wait_ge(*finished("act", s.after))
                    pool.wait_ge(*finished("dve", s.after))
                if k in ("sq", "sk"):
                    pool.wait_ge(sems["dve_rope"], value("dve_rope", s, 5))
                    dst = swa["sq_s"][:, 2 * s.j:2 * s.j + 2, 0:NLAT] if k == "sq" else swa["sk_s"][:, :, 0:NLAT]
                    gp.tensor_tensor(dst, swa["rp"][:, 0], swa["rp"][:, 1], ALU.add).then_inc(sems["pool_evac"], 1)
                elif k == "uqp":
                    pool.wait_ge(sems["dve_rope"], value("dve_rope", s, 3))
                    gp.tensor_tensor(mla["qp"][:, 0:NLAT], mla["mla_p"][:, 0, 0:NLAT], mla["mla_p"][:, 1, 0:NLAT], ALU.add).then_inc(sems["pool_evac"], 1)
                elif k == "branch":
                    pool.wait_ge(sems["dve_evac"], value("dve_evac", s, 1))
                    dst = mg[:, 2 * s.j:2 * s.j + 2, :s.t]
                    gp.tensor_tensor(dst, dst, br["bt"][:, s.j % 2, :, :s.t], ALU.add).then_inc(sems["pool_evac"], 1)
                elif k == "squares":
                    pool.wait_ge(sems["x_in"], 16)
                    pool.wait_ge(*finished("dve", s.after))
                    pool.wait_ge(*finished("pe", s.after))
                    pool.wait_ge(*finished("act", s.after))
                    done = 0
                    for c in (2 * s.j, 2 * s.j + 1):
                        place = sums["sq"][:, 2, :s.tn] if c else sums["total"][:, :s.tn]
                        gp.tensor_tensor(place, x[:, c, :s.tn], x[:, c, :s.tn], ALU.mult).then_inc(sems["norm_partial"], 1)
                        done += 1
                        pool.wait_ge(sems["norm_partial"], value("norm_partial", s, done))
                        if c:
                            gp.tensor_tensor(sums["total"][:, :s.tn], sums["total"][:, :s.tn], place, ALU.add).then_inc(sems["norm_partial"], 1)
                            done += 1
                            pool.wait_ge(sems["norm_partial"], value("norm_partial", s, done))
                elif k == "norm":
                    pool.wait_ge(*finished("pe", s.i - 1))
                    pool.wait_ge(sems["norm_inverse"], value("norm_inverse", s, 1))
                    for c in range(1, KC, 2):
                        gp.tensor_tensor(nrm["xn"][:, c, :s.tn], x[:, c, :s.tn], nrm["rinv"][:, :s.tn], ALU.mult).then_inc(sems["norm_scaled_odd"], 1)
                elif k in ("gla1", "gla2"):
                    before_it = s.i - 1 if s.h == 0 and k == "gla1" else s.needs
                    pool.wait_ge(*finished("pe", before_it))
                    pool.wait_ge(*finished("act", before_it))
                    pool.wait_ge(*finished("dve", before_it))
                    h2 = s.h % 2
                    if k == "gla1":
                        gp.memset(gla["at"][:], 0.0).then_inc(sems["gla_zeroed"], 1)
                        gp.memset(gla["ktp"][:], 0.0).then_inc(sems["gla_zeroed"], 1)
                    else:
                        for d in range(2):
                            pool.wait_ge(sems["gla_exps"], value("gla_exps", s, 2 * (d + 1)))
                            gp.tensor_tensor(gla["qd"][:, d, :s.tq], gla["gq_s"][:, h2, :s.tq], gla["ep"][:, d, :s.tq], ALU.mult)\
                                .then_inc(sems["gla_qdec"], 1)
                        for d in range(2):
                            pool.wait_ge(sems["gla_exp_end"], value("gla_exp_end", s, d + 1))
                            gp.tensor_tensor(gla["ke"][:, d, :], gla["gk_s"][:, h2, :], gla["ke"][:, d, :], ALU.mult)\
                                .then_inc(sems["gla_kend"], 1)
                elif k == "krope":
                    pool.wait_ge(*finished("pe", s.i - 1))
                    pool.wait_ge(*finished("act", s.i - 1))
                    pool.wait_ge(*finished("dve", s.i - 1))
                    pool.wait_ge(*finished("pool", s.i - 1))
                    for a in range(2):
                        rows = slice(64 * (1 - a), 64 * (1 - a) + 64)
                        gp.memset(kpe[rows, a, :], 0.0).then_inc(sems["lat_zeroed"], 1)
                    pool.wait_ge(sems["lat_rope"], value("lat_rope", s, 3))
                    for a in range(2):
                        rows = slice(64 * a, 64 * a + 64)
                        gp.tensor_tensor(kpe[rows, a, 0:NLAT], lat["cx_sq"][rows, 2, 0:NLAT], lat["cx_sq"][rows, 3, 0:NLAT], ALU.add).then_inc(sems["lat_k_roped"], 1)


def constants():
    c = np.zeros((P, NCONST), np.float32)
    c[:, CONST["ident"]] = np.eye(P)
    c[:, CONST["ones"]] = 1.0
    t = np.arange(P)
    same = t[:, None] // GLA_CHUNK == t[None, :] // GLA_CHUNK
    c[:, CONST["tri"]] = np.concatenate([same & (t[:, None] <= t), same & (t[:, None] >= t)], 1) / 16.0
    c[:, CONST["band"]] = np.where(np.concatenate([t <= t[:, None], t >= t[:, None]], 1), 0.0, NEG)
    row, col = np.arange(NLAT) // 64, np.arange(NLAT) % 64

    def tables(half):
        inv = np.float32(10000.0) ** (-np.arange(0, 2 * half, 2, dtype=np.float32) / np.float32(2 * half))
        angle = [(inv[:, None] * pos.astype(np.float32)).astype(np.float32) for pos in (row, col)]
        cos = np.concatenate([np.cos(a) for a in angle for _ in range(2)])
        sin = np.concatenate([s * np.sin(a) for a in angle for s in (-1, 1)])
        return cos.astype(np.float32), sin.astype(np.float32)

    cos, sin = tables(32)
    c[:, CONST["swa_cos"]] = cos
    c[:, CONST["swa_sin"]] = sin.reshape(4, 32, NLAT)[[1, 0, 3, 2]].reshape(P, NLAT)
    cos, sin = tables(16)
    c[:, CONST["mla_cos"]] = np.concatenate([cos, cos])
    c[:, CONST["mla_sin"]] = np.concatenate([sin, sin])
    return c


def weight_block(b, w):
    l, j = b.layer, b.j
    win = w["w_in"][l]

    def cols(name, n, width=256):
        return win[:, OFF[name] + n * width:OFF[name] + (n + 1) * width]

    if b.name == "ada":
        m = w["ada_w"][l][:, j * 256:(j + 1) * 256]
    elif b.name == "zk":
        kr = cols("kr", 0, 64)
        m = np.concatenate([cols("gzf", 0, 32), np.zeros((D, 96), win.dtype), kr, kr], 1)
    elif b.name == "cq":
        m = (cols("cq", 0), cols("ckv", 0), cols("cq", 2, 128))[j]
    elif b.name == "gq":
        m = np.concatenate([cols("gq", j, 128), cols("gk", j, 128)], 1)
    elif b.name in OFF:
        m = cols(b.name, j)
    elif b.name == "gate":
        m = cols("gates", 4 * b.part + j)
    elif b.name == "branch":
        m = w["w_branch"][l, b.part][:, j * 256:(j + 1) * 256]
    elif b.name == "out":
        m = w["w_out"][l][:, j * 256:(j + 1) * 256]
    elif b.name == "up":
        m = w["mlp_w1"][l][:, b.part * QUARTER + j * 256:b.part * QUARTER + (j + 1) * 256]
    elif b.name == "down":
        m = w["mlp_w2"][l][b.part * QUARTER:(b.part + 1) * QUARTER, j * 256:(j + 1) * 256]
    elif b.name == "ukn":
        m = w["mla_w_ukv"][l].reshape(MLA_KV, 8, 2, HEAD)[:, 2 * j:2 * j + 2].transpose(0, 2, 1, 3).reshape(MLA_KV, 512)
    else:
        h = w["mla_w_uq"][l].reshape(MLA_Q, 8, 192)[:, 2 * j:2 * j + 2]
        m = np.concatenate([h[:, 0, :HEAD], h[:, 1, :HEAD], h[:, 0, HEAD:], h[:, 1, HEAD:]], 1)
    return m.reshape(-1, P, m.shape[1]).transpose(1, 0, 2)


def chunked(v):
    return v.reshape(-1, P).T


def kernel(**inputs):
    import concourse.bacc as bacc
    from concourse.bass_utils import run_bass_kernel_spmd

    w = {k: np.asarray(v) for k, v in inputs.items()}
    tokens = np.concatenate([w["x"][0], w["ctx"][0]], 0)
    cvec = np.zeros((P, KC, 32), np.float32)
    cvec[:, :, 0] = chunked(w["c"][0])
    cvec[:, :, 1] = chunked(w["c_ctx"])
    vectors = np.zeros((P, NVEC), np.float32)
    decay = np.zeros((DEPTH, P, 2, 512), np.float32)
    for l in range(DEPTH):
        for name, key in (("mix", "norm_mix_w"), ("mlp", "norm_mlp_w"), ("ada_b", "ada_b"), ("gla", "gla_norm_w"),
                          ("mq", "mla_q_norm_w"), ("mkv", "mla_kv_norm_w")):
            vectors[:, VEC[name, l]] = chunked(w[key][l])
        vectors[:, VEC["sink", l]] = w["swa_sink"][l][None, :]
        for d in range(2):
            decay[l, d * GLA_RANK:(d + 1) * GLA_RANK, d] = w["gla_a_w"][l, d]
            decay[l, 2 * GLA_RANK, d] = w["gla_a_b"][l, d]
    vectors[:, VEC["final", 0]] = chunked(w["final_norm_w"])
    _, blocks = plan()
    weights = np.empty(P * sum(b.size for b in blocks), np.float32)
    at = 0
    for b in blocks:
        m = weight_block(b, w)
        assert m.shape[1] * m.shape[2] == b.size, (b, m.shape)
        weights[at:at + m.size].reshape(m.shape)[...] = m
        at += m.size
    arrays = dict(xt=np.ascontiguousarray(tokens.T.reshape(KC, P, T).transpose(1, 0, 2)), cvec=cvec, consts=constants(),
                  vectors=vectors, decay_w=decay, weights=weights)

    nc = bacc.Bacc("TRN2", target_bir_lowering=False, num_devices=1)
    args = {n: nc.dram_tensor(n, a.shape, F32, kind="ExternalInput").ap() for n, a in arrays.items()}
    out = nc.dram_tensor("out", (P, KC, NLAT), F32, kind="ExternalOutput").ap()
    build(nc, out=out, **args)
    r = run_bass_kernel_spmd(nc, [arrays], core_ids=[0])
    got = r.results[0]["out"]
    return got.transpose(1, 0, 2).reshape(D, NLAT).T.reshape(1, NLAT, D)
```
